# Optimizing a Trainium2 kernel written in Bass

```python
import jax, jax.numpy as jnp
from jax import lax
import numpy as np

D_MODEL = 1024
BATCH = 1
SEQ = 512
DEPTH = 2
DEC_BATCH = 8
DEC_SEQ = 1
PAST_LEN = 2048
PAGE_SIZE = 128

RET_HEADS = 4
RET_DK = 64
RET_DV = 64
RET_CHUNK = 128
MLA_HEADS = 8
MLA_NOPE = 64
MLA_ROPE = 32
MLA_V = 64
MLA_Q_RANK = 256
MLA_KV_RANK = 128
MLA_Q_BLOCK = 128
MLA_SCALE = (MLA_NOPE + MLA_ROPE) ** -0.5
RG_WIDTH = 256
RG_BLOCKS = 4
RG_CONV = 4
RG_C = 8.0
D_FF = 2816
FFN_CONV = 3
ROPE_BASE = 10000.0
EPS = 1e-6
NEG_INF = -1e30
MIX_WIDTH = RET_HEADS * RET_DV + MLA_HEADS * MLA_V + RG_WIDTH
IN_SIZES = (RET_HEADS * RET_DK, RET_HEADS * RET_DK, RET_HEADS * RET_DV, RET_HEADS * RET_DV,
            MLA_Q_RANK, MLA_KV_RANK, MLA_ROPE, RG_WIDTH, RG_WIDTH)
N_IN = sum(IN_SIZES)

kernel_name = 'hymba_retention_mla_rglru_convffn_step'

def rmsnorm(x, w):
    xf = x.astype(jnp.float32)
    y = xf * lax.rsqrt(jnp.mean(xf * xf, axis=-1, keepdims=True) + EPS)
    return (y * w.astype(jnp.float32)).astype(x.dtype)

def rope(x, pos):
    half = x.shape[-1] // 2
    freqs = ROPE_BASE ** (-jnp.arange(half, dtype=jnp.float32) / half)
    ang = pos[:, None] * freqs[None, :]
    cos = jnp.cos(ang)[:, None, :]
    sin = jnp.sin(ang)[:, None, :]
    xf = x.astype(jnp.float32)
    x1, x2 = xf[..., :half], xf[..., half:]
    return jnp.concatenate([x1 * cos - x2 * sin, x1 * sin + x2 * cos], axis=-1).astype(x.dtype)

def causal_dwconv(buf, x, w, b):
    width = w.shape[0]
    T = x.shape[1]
    xp = jnp.concatenate([buf.astype(x.dtype), x], axis=1)
    y = b + xp[:, 0:T] * w[0]
    for k in range(1, width):
        y = y + xp[:, k:k + T] * w[k]
    return y, xp[:, xp.shape[1] - (width - 1):]

def retention_log_gamma():
    return jnp.log(1.0 - 2.0 ** (-5.0 - jnp.arange(RET_HEADS, dtype=jnp.float32)))

def retention_chunk(q, k, v, S0, log_gamma):
    L = q.shape[1]
    idx = jnp.arange(L, dtype=jnp.float32)
    rel = idx[:, None] - idx[None, :]
    decay = jnp.where(rel >= 0, jnp.exp(log_gamma[:, None, None] * jnp.maximum(rel, 0.0)), 0.0)
    s = jnp.einsum('blhd,bmhd->bhlm', q, k) * decay
    inner = jnp.einsum('bhlm,bmhe->blhe', s, v)
    cross = jnp.einsum('blhd,bhde->blhe', q, S0) * jnp.exp(log_gamma[None, :] * (idx[:, None] + 1.0))[None, :, :, None]
    wk = jnp.exp(log_gamma[None, :] * (L - 1.0 - idx[:, None]))
    S = jnp.exp(log_gamma * L)[None, :, None, None] * S0 + jnp.einsum('blhd,blhe,lh->bhde', k, v, wk)
    return inner + cross, S

def retention_mixer(q, k, v, S0, pos):
    B, T = q.shape[0], q.shape[1]
    q = rope(q, pos).astype(jnp.float32)
    k = rope(k, pos).astype(jnp.float32) * (RET_DK ** -0.5)
    v = v.astype(jnp.float32)
    S0 = S0.astype(jnp.float32)
    lg = retention_log_gamma()
    if T > RET_CHUNK and T % RET_CHUNK == 0:
        n = T // RET_CHUNK

        def to_chunks(a):
            return a.reshape(B, n, RET_CHUNK, *a.shape[2:]).swapaxes(0, 1)

        def step(S, qkv):
            o, S_next = retention_chunk(qkv[0], qkv[1], qkv[2], S, lg)
            return S_next, o

        S_fin, o = lax.scan(step, S0, (to_chunks(q), to_chunks(k), to_chunks(v)))
        o = o.swapaxes(0, 1).reshape(B, T, RET_HEADS, RET_DV)
    else:
        o, S_fin = retention_chunk(q, k, v, S0, lg)
    return o, S_fin

def retention_out(o, g, gn_w):
    B, T, H, E = o.shape
    mu = jnp.mean(o, axis=-1, keepdims=True)
    var = jnp.mean(jnp.square(o - mu), axis=-1, keepdims=True)
    on = ((o - mu) * lax.rsqrt(var + EPS)).reshape(B, T, H * E) * gn_w.astype(jnp.float32)
    return on.astype(g.dtype) * jax.nn.silu(g)

def mla_project(cq, ckv, kr, pos, q_norm_w, w_uq, kv_norm_w, w_uk):
    cq = rmsnorm(cq, q_norm_w)
    q = jnp.einsum('btr,rhd->bthd', cq, w_uq)
    q_nope, q_rope = q[..., :MLA_NOPE], q[..., MLA_NOPE:]
    q_rope = rope(q_rope, pos) * MLA_SCALE
    ckv = rmsnorm(ckv, kv_norm_w)
    k_rope = rope(kr[:, :, None, :], pos)[:, :, 0]
    q_lat = jnp.einsum('bthd,rhd->bthr', q_nope, w_uk) * MLA_SCALE
    return q_lat, q_rope, ckv, k_rope

def mla_attend_causal(q_lat, q_rope, ckv, k_rope):
    B, S, H, R = q_lat.shape
    nb = S // MLA_Q_BLOCK
    kpos = jnp.arange(S)

    def blk(args):
        ql, qr, start = args
        s = (jnp.einsum('bqhr,bkr->bhqk', ql, ckv) + jnp.einsum('bqhd,bkd->bhqk', qr, k_rope)).astype(jnp.float32)
        qpos = start + jnp.arange(MLA_Q_BLOCK)
        s = jnp.where(kpos[None, :] <= qpos[:, None], s, NEG_INF)
        p = jax.nn.softmax(s, axis=-1).astype(ckv.dtype)
        return jnp.einsum('bhqk,bkr->bqhr', p, ckv)

    qlb = q_lat.reshape(B, nb, MLA_Q_BLOCK, H, R).swapaxes(0, 1)
    qrb = q_rope.reshape(B, nb, MLA_Q_BLOCK, H, MLA_ROPE).swapaxes(0, 1)
    out = lax.map(blk, (qlb, qrb, jnp.arange(nb) * MLA_Q_BLOCK))
    return out.swapaxes(0, 1).reshape(B, S, H, R)

def mla_attend_paged(q_lat, q_rope, ckv, k_rope, pool_lat, pool_rope, page_table):
    DB, T, H, R = q_lat.shape
    past_lat = pool_lat[page_table].reshape(DB, -1, R)
    past_rope = pool_rope[page_table].reshape(DB, -1, MLA_ROPE)
    P = past_lat.shape[1]
    s_past = jnp.einsum('bqhr,bkr->bhqk', q_lat, past_lat) + jnp.einsum('bqhd,bkd->bhqk', q_rope, past_rope)
    s_new = jnp.einsum('bqhr,bkr->bhqk', q_lat, ckv) + jnp.einsum('bqhd,bkd->bhqk', q_rope, k_rope)
    causal = jnp.arange(T)[None, :] <= jnp.arange(T)[:, None]
    s_new = jnp.where(causal, s_new.astype(jnp.float32), NEG_INF)
    s = jnp.concatenate([s_past.astype(jnp.float32), s_new], axis=-1)
    p = jax.nn.softmax(s, axis=-1)
    p_past = p[..., :P].astype(ckv.dtype)
    p_new = p[..., P:].astype(ckv.dtype)
    return jnp.einsum('bhqk,bkr->bqhr', p_past, past_lat) + jnp.einsum('bhqk,bkr->bqhr', p_new, ckv)

def rglru_mixer(xb, gb, buf0, h0, conv_w, conv_b, w_a, b_a, w_x, b_x, lam):
    xc, buf = causal_dwconv(buf0, xb, conv_w, conv_b)
    B, T, _ = xc.shape
    xr = xc.reshape(B, T, RG_BLOCKS, RG_WIDTH // RG_BLOCKS)
    r = jax.nn.sigmoid((jnp.einsum('btnc,ncd->btnd', xr, w_a).reshape(B, T, RG_WIDTH) + b_a).astype(jnp.float32))
    i = jax.nn.sigmoid((jnp.einsum('btnc,ncd->btnd', xr, w_x).reshape(B, T, RG_WIDTH) + b_x).astype(jnp.float32))
    log_a = -RG_C * r * jax.nn.softplus(-lam.astype(jnp.float32))
    a = jnp.exp(log_a)
    u = jnp.sqrt(-jnp.expm1(2.0 * log_a)) * i * xc.astype(jnp.float32)
    u = u.at[:, 0].add(a[:, 0] * h0.astype(jnp.float32))

    def comb(left, right):
        return left[0] * right[0], right[0] * left[1] + right[1]

    _, h = lax.associative_scan(comb, (a, u), axis=1)
    out = h.astype(xb.dtype) * jax.nn.gelu(gb)
    return out, buf, h[:, -1]

def conv_ffn(h, buf0, w_up, conv_w, conv_b, w_down):
    up = h @ w_up
    gate, val = up[..., :D_FF], up[..., D_FF:]
    gc, buf = causal_dwconv(buf0, gate, conv_w, conv_b)
    return (jax.nn.silu(gc) * val) @ w_down, buf

def layer(x, pos, l, P, ret_S0, rg_buf0, rg_h0, ffn_buf0, attend):
    B, T, _ = x.shape
    h = rmsnorm(x, P['norm1_w'][l])
    z = h @ P['w_in'][l]
    rq, rk, rv, rgate, cq, ckv, kr, gx, gg = jnp.split(z, [int(c) for c in np.cumsum(IN_SIZES)[:-1]], axis=-1)
    o_ret, S_ret = retention_mixer(rq.reshape(B, T, RET_HEADS, RET_DK), rk.reshape(B, T, RET_HEADS, RET_DK),
                                   rv.reshape(B, T, RET_HEADS, RET_DV), ret_S0, pos)
    y_ret = retention_out(o_ret, rgate, P['ret_gn_w'][l])
    q_lat, q_rope, ckv, k_rope = mla_project(cq, ckv, kr, pos, P['mla_q_norm_w'][l], P['mla_w_uq'][l],
                                             P['mla_kv_norm_w'][l], P['mla_w_uk'][l])
    o_lat = attend(l, q_lat, q_rope, ckv, k_rope)
    y_mla = jnp.einsum('bthr,rhd->bthd', o_lat, P['mla_w_uv'][l]).reshape(B, T, MLA_HEADS * MLA_V)
    y_rg, rg_buf, rg_h = rglru_mixer(gx, gg, rg_buf0, rg_h0, P['rg_conv_w'][l], P['rg_conv_b'][l],
                                     P['rg_w_a'][l], P['rg_b_a'][l], P['rg_w_x'][l], P['rg_b_x'][l],
                                     P['rg_lambda'][l])
    x = x + jnp.concatenate([y_ret, y_mla, y_rg], axis=-1) @ P['w_out'][l]
    f, ffn_buf = conv_ffn(rmsnorm(x, P['norm2_w'][l]), ffn_buf0, P['ffn_w_up'][l], P['ffn_conv_w'][l],
                          P['ffn_conv_b'][l], P['ffn_w_down'][l])
    x = x + f
    return x, (ckv, k_rope, S_ret, rg_buf, rg_h, ffn_buf)

def run_trunk(x, pos, P, ret_S, rg_buf, rg_h, ffn_buf, attend):
    news = []
    for l in range(DEPTH):
        x, st = layer(x, pos, l, P, ret_S[l], rg_buf[l], rg_h[l], ffn_buf[l], attend)
        news.append(st)
    y = rmsnorm(x, P['final_norm_w'])
    stacked = [jnp.stack([s[i] for s in news]) for i in range(6)]
    return y, stacked

def setup_inputs(seed: int = 0) -> dict:
    key = jax.random.key(seed)
    ks = iter(jax.random.split(key, 40))
    n_pages = PAST_LEN // PAGE_SIZE
    n_phys = (DEC_BATCH * n_pages * 5) // 4

    def nrm(shape, scale=1.0):
        return jax.random.normal(next(ks), shape, jnp.float32) * scale

    x_prompt = nrm((BATCH, SEQ, D_MODEL))
    x_sample = nrm((DEC_BATCH, DEC_SEQ, D_MODEL))
    cache_mla_latent = nrm((DEPTH, n_phys, PAGE_SIZE, MLA_KV_RANK))
    cache_mla_krope = nrm((DEPTH, n_phys, PAGE_SIZE, MLA_ROPE))
    page_table = jax.random.permutation(next(ks), n_phys)[:DEC_BATCH * n_pages].reshape(DEC_BATCH, n_pages).astype(jnp.int32)
    state_ret = nrm((DEPTH, DEC_BATCH, RET_HEADS, RET_DK, RET_DV))
    state_rg_conv = nrm((DEPTH, DEC_BATCH, RG_CONV - 1, RG_WIDTH))
    state_rglru = nrm((DEPTH, DEC_BATCH, RG_WIDTH), 0.5)
    state_ffn_conv = nrm((DEPTH, DEC_BATCH, FFN_CONV - 1, D_FF))
    bw = RG_WIDTH // RG_BLOCKS
    u = jax.random.uniform(next(ks), (DEPTH, RG_WIDTH), jnp.float32, 0.9, 0.999)
    a_base = u ** (1.0 / RG_C)
    rg_lambda = jnp.log(a_base) - jnp.log1p(-a_base)
    return {
        'x_prompt': x_prompt,
        'x_sample': x_sample,
        'cache_mla_latent': cache_mla_latent,
        'cache_mla_krope': cache_mla_krope,
        'page_table': page_table,
        'state_ret': state_ret,
        'state_rg_conv': state_rg_conv,
        'state_rglru': state_rglru,
        'state_ffn_conv': state_ffn_conv,
        'norm1_w': 1.0 + nrm((DEPTH, D_MODEL), 0.01),
        'w_in': nrm((DEPTH, D_MODEL, N_IN), D_MODEL ** -0.5),
        'ret_gn_w': 1.0 + nrm((DEPTH, RET_HEADS * RET_DV), 0.01),
        'mla_q_norm_w': 1.0 + nrm((DEPTH, MLA_Q_RANK), 0.01),
        'mla_w_uq': nrm((DEPTH, MLA_Q_RANK, MLA_HEADS, MLA_NOPE + MLA_ROPE), MLA_Q_RANK ** -0.5),
        'mla_kv_norm_w': 1.0 + nrm((DEPTH, MLA_KV_RANK), 0.01),
        'mla_w_uk': nrm((DEPTH, MLA_KV_RANK, MLA_HEADS, MLA_NOPE), MLA_KV_RANK ** -0.5),
        'mla_w_uv': nrm((DEPTH, MLA_KV_RANK, MLA_HEADS, MLA_V), MLA_KV_RANK ** -0.5),
        'rg_conv_w': nrm((DEPTH, RG_CONV, RG_WIDTH), RG_CONV ** -0.5),
        'rg_conv_b': nrm((DEPTH, RG_WIDTH), 0.01),
        'rg_w_a': nrm((DEPTH, RG_BLOCKS, bw, bw), bw ** -0.5),
        'rg_b_a': nrm((DEPTH, RG_WIDTH), 0.01),
        'rg_w_x': nrm((DEPTH, RG_BLOCKS, bw, bw), bw ** -0.5),
        'rg_b_x': nrm((DEPTH, RG_WIDTH), 0.01),
        'rg_lambda': rg_lambda,
        'w_out': nrm((DEPTH, MIX_WIDTH, D_MODEL), MIX_WIDTH ** -0.5),
        'norm2_w': 1.0 + nrm((DEPTH, D_MODEL), 0.01),
        'ffn_w_up': nrm((DEPTH, D_MODEL, 2 * D_FF), D_MODEL ** -0.5),
        'ffn_conv_w': nrm((DEPTH, FFN_CONV, D_FF), FFN_CONV ** -0.5),
        'ffn_conv_b': nrm((DEPTH, D_FF), 0.01),
        'ffn_w_down': nrm((DEPTH, D_FF, D_MODEL), D_FF ** -0.5),
        'final_norm_w': 1.0 + nrm((D_MODEL,), 0.01),
    }

def reference(x_prompt, x_sample, cache_mla_latent, cache_mla_krope, page_table, state_ret, state_rg_conv,
              state_rglru, state_ffn_conv, norm1_w, w_in, ret_gn_w, mla_q_norm_w, mla_w_uq, mla_kv_norm_w,
              mla_w_uk, mla_w_uv, rg_conv_w, rg_conv_b, rg_w_a, rg_b_a, rg_w_x, rg_b_x, rg_lambda, w_out,
              norm2_w, ffn_w_up, ffn_conv_w, ffn_conv_b, ffn_w_down, final_norm_w):
    P = dict(norm1_w=norm1_w, w_in=w_in, ret_gn_w=ret_gn_w, mla_q_norm_w=mla_q_norm_w, mla_w_uq=mla_w_uq,
             mla_kv_norm_w=mla_kv_norm_w, mla_w_uk=mla_w_uk, mla_w_uv=mla_w_uv, rg_conv_w=rg_conv_w,
             rg_conv_b=rg_conv_b, rg_w_a=rg_w_a, rg_b_a=rg_b_a, rg_w_x=rg_w_x, rg_b_x=rg_b_x,
             rg_lambda=rg_lambda, w_out=w_out, norm2_w=norm2_w, ffn_w_up=ffn_w_up, ffn_conv_w=ffn_conv_w,
             ffn_conv_b=ffn_conv_b, ffn_w_down=ffn_w_down, final_norm_w=final_norm_w)

    B, S, _ = x_prompt.shape
    pos_p = jnp.arange(S, dtype=jnp.float32)
    zeros_ret = jnp.zeros((DEPTH, B, RET_HEADS, RET_DK, RET_DV), jnp.float32)
    zeros_rgc = jnp.zeros((DEPTH, B, RG_CONV - 1, RG_WIDTH), x_prompt.dtype)
    zeros_rgh = jnp.zeros((DEPTH, B, RG_WIDTH), jnp.float32)
    zeros_ffc = jnp.zeros((DEPTH, B, FFN_CONV - 1, D_FF), x_prompt.dtype)

    def attend_prompt(l, ql, qr, c, k):
        return mla_attend_causal(ql, qr, c, k)

    y_prompt, (p_lat, p_rope, p_ret, p_rgc, p_rgh, p_ffc) = run_trunk(
        x_prompt, pos_p, P, zeros_ret, zeros_rgc, zeros_rgh, zeros_ffc, attend_prompt)

    T = x_sample.shape[1]
    pos_s = PAST_LEN + jnp.arange(T, dtype=jnp.float32)

    def attend_sample(l, ql, qr, c, k):
        return mla_attend_paged(ql, qr, c, k, cache_mla_latent[l], cache_mla_krope[l], page_table)

    y_sample, (s_lat, s_rope, s_ret, s_rgc, s_rgh, s_ffc) = run_trunk(
        x_sample, pos_s, P, state_ret, state_rg_conv, state_rglru, state_ffn_conv, attend_sample)

    return (y_prompt, y_sample, p_lat, p_rope, p_ret, p_rgc, p_rgh, p_ffc,
            s_lat, s_rope, s_ret, s_rgc, s_rgh, s_ffc)


_drawn_inputs = setup_inputs


def setup_inputs(seed=0):
    import zlib

    import numpy as np

    out = dict(_drawn_inputs(seed))
    spreads = {}
    factors = {'cache_mla_krope': 3.115,
     'norm1_w': 3.447,
     'ret_gn_w': 8.0,
     'mla_q_norm_w': 8.0,
     'mla_kv_norm_w': 6.031,
     'rg_b_a': 30.584,
     'rg_b_x': 29.509,
     'norm2_w': 4.627,
     'ffn_conv_b': 7.835,
     'final_norm_w': 29.619,
     'rg_conv_b': 3.204}
    for name, (base, spread) in spreads.items():
        noise = np.random.default_rng([zlib.crc32(name.encode()), seed]).standard_normal(out[name].shape)
        drawn = base * np.exp(spread * noise) if base else spread * noise
        out[name] = __import__('jax').numpy.asarray(drawn.astype(out[name].dtype))
    for name, factor in factors.items():
        out[name] = (out[name] * factor).astype(out[name].dtype)
    return out
```

```python
from contextlib import ExitStack

import concourse.bass as bass
import numpy as np
from concourse import mybir

F32 = mybir.dt.float32
F32R = mybir.dt.float32r
I32 = mybir.dt.int32
ACT = mybir.ActivationFunctionType
ALU = mybir.AluOpType
AX = mybir.AxisListType.X

P = 128
D_MODEL, SEQ, DEPTH, NB = 1024, 512, 2, 8
T = SEQ + NB
HB = T // 2
KD = D_MODEL // P
PAGE, N_PAGES, N_PHYS, PAST = 128, 16, 160, 2048
RH, HD = 4, 64
MH, ROPE_D, KVR, QR_ = 8, 32, 128, 256
RG, RGC = 2, 4
D_FF = 2816
NJ = D_FF // P
EPS = 1e-6
SCALE = (64 + 32) ** -0.5
NEG = -1e30
G_C1, G_C2 = 0.044715, float(np.sqrt(2.0 / np.pi))
HALVES = ((0, 12), (12, 10))

Z_CKV, Z_CQ, Z_RQ, Z_KR, Z_RK, Z_RV, Z_GX, Z_GG, Z_GATE = 0, (1, 2), (3, 5), 4, (6, 7), (8, 9), (10, 11), (12, 13), (14, 15)
N_IN_U = 16
U_OUT = N_IN_U
U_UP = [0, 0]
U_DN = [0, 0]
U_UP[0] = U_OUT + KD
U_DN[0] = U_UP[0] + 2 * HALVES[0][1]
U_UP[1] = U_DN[0] + 2 * KD
U_DN[1] = U_UP[1] + 2 * HALVES[1][1]
N_UNITS = U_DN[1] + 2 * KD
NRAW, NHL = 4, 2
UW = KD * P

DECODE_TILES = [["ds6", "ds7"], ["dn", "dm"], ["db"], ["dd"], ["dp0", "dp1"], ["dp2", "dp3"], ["dp4", "dp5"],
                ["dp6", "dp7"], ["dy"]]
TILES = ["n1"] + [f"in{u}" for u in range(5)] + ["nckv", "ncq"] + [f"in{u}" for u in range(5, 16)]
TILES += ["pkr"] + [f"pz{i}" for i in range(4)]
TILES += ["q8", "pq8", "ql", "ds0", "ds1"]
TILES += ["g0r", "g0i", "g1r", "g1i"]
TILES += ["rt0", "rt1", "rs0", "rs1", "kv", "ds2", "ds3", "ro", "dk", "du", "do"]
TILES += ["gm0", "gm1", "ds4", "ds5", "gv0", "gv1"]
TILES += ["qr0", "pqr0", "qr1", "pqr1", "v01", "v23"]
for _h in range(MH + 1):
    if _h < MH:
        if _h % 2 == 0:
            TILES += [f"q{_h // 2}", f"k{_h // 2}"]
        TILES += [f"sA{_h}", f"sB{_h}"]
    if _h:
        TILES += [f"tA{_h - 1}", f"tB{_h - 1}", f"o{_h - 1}"]
    TILES += DECODE_TILES[_h]
TILES += [f"wo{m}" for m in range(KD)] + ["n2"]
for _i, (_j0, _n) in enumerate(HALVES):
    TILES += [f"up{_i}_{j}" for j in range(2 * _n)] + [f"dn{_i}_{m}" for m in range(KD)]
assert len(TILES) % 4 == 0
TILE_AT = {name: i for i, name in enumerate(TILES)}
NT4 = len(TILES) // 4

SQ_USES = [("n1", k, KD) for k in range(KD)] + [("nckv", 0, 1), ("ncq", 0, 2), ("ncq", 1, 2)]
SQ_USES += [("gv0", 0, 1), ("gv1", 0, 1)] + [("n2", k, KD) for k in range(KD)]
SQ_MID = [sum(k < n - 1 for _, k, n in SQ_USES[:i]) for i in range(len(SQ_USES) + 1)]

CONST_W = [("ident", 128), ("ones", 128), ("bd64", 128), ("perm64", 128), ("perm32", 128),
           ("cosr", T), ("sinr", T), ("cosm", T), ("sinm", T), ("decay", 512), ("gq", 256), ("wk", 256),
           ("gam", 4), ("causal", 128), ("newmask", 64), ("bmask", 512), ("zero", 4)]
CONST_AT, _o = {}, 0
for _n_, _w in CONST_W:
    CONST_AT[_n_] = (_o, _w)
    _o += _w
CONST_N = _o
PAR_W = [("n1", 8), ("n2", 8), ("qn", 2), ("kn", 1), ("gn", 2), ("rcw", 8), ("rcb", 2), ("ba", 2), ("bx", 2),
         ("lam", 2), ("fcw", 3 * NJ), ("fcb", NJ), ("cbuf", 48), ("h0", 16), ("fbuf", NJ * 16), ("fin", 8)]
PAR_AT, _o = {}, 0
for _n_, _w in PAR_W:
    PAR_AT[_n_] = (_o, _w)
    _o += _w
PAR_N = _o


def constants():
    c = {n: np.zeros((P, w), np.float32) for n, w in CONST_W}
    f32 = np.float32
    pos = np.concatenate([np.arange(SEQ), np.full(NB, PAST)]).astype(f32)
    p = np.arange(P)
    c["ident"][:] = np.eye(P)
    c["ones"][:] = 1.0
    c["bd64"][:] = np.kron(np.eye(2), np.ones((64, 64))) / 64.0
    for name, half, cn, sn in (("perm64", 32, "cosr", "sinr"), ("perm32", 16, "cosm", "sinm")):
        c[name][p ^ half, p] = 1.0
        freqs = (f32(10000.0) ** (-np.arange(half, dtype=f32) / f32(half))).astype(f32)
        ang = (pos[None, :] * freqs[p % half][:, None]).astype(f32)
        c[cn][:] = np.cos(ang)
        c[sn][:] = np.where((p // half % 2 == 0)[:, None], -np.sin(ang), np.sin(ang))
    lg = np.log(1.0 - 2.0 ** (-5.0 - np.arange(RH)))
    i = np.arange(P)
    rel = i[None, :] - i[:, None]
    for h in range(RH):
        o = (2 * (h % 2) + h // 2) * P
        c["decay"][:, o:o + P] = np.where(rel >= 0, np.exp(lg[h] * np.maximum(rel, 0)), 0)
        c["wk"][:, h * HD:(h + 1) * HD] = np.exp(lg[h] * (P - 1.0 - i))[:, None]
        rows = slice(64 * (h % 2), 64 * (h % 2) + 64)
        c["gq"][rows, (h // 2) * P:(h // 2 + 1) * P] = np.exp(lg[h] * (i + 1.0))[None]
        c["gam"][rows, h // 2] = np.exp(lg[h] * P)
        c["gam"][rows, 2 + h // 2] = np.exp(lg[h])
    c["causal"][:] = np.where(i[None, :] <= i[:, None], 0.0, NEG)
    b = np.arange(NB)
    c["newmask"][:NB] = np.where(np.repeat(b, MH)[None] == b[:, None], 0.0, NEG)
    c["bmask"][:NB] = (np.repeat(b, HD)[None] == b[:, None])
    return np.concatenate([c[n] for n, _ in CONST_W], 1)


def build(nc, units, constd, pard, xd, uqd, ukd, uktd, uvd, wgd, s0d, katd, karp, kav, ptd, cpd, fpd,
          y_o, lat_o, rope_o, pret_o, gx_o, hr_o, ff_o, sret_o, rgc0_o, ffc0_o):
    ctx = ExitStack()
    with ctx:
        sem = lambda name: ctx.enter_context(nc.semaphore(name))
        cursor = [(nc.sbuf_base + 31) // 32 * 32]

        def over(name, shape, dt=F32, at=None):
            size = (4 * int(np.prod(shape[1:])) + 31) // 32 * 32
            o = cursor[0] if at is None else at
            if at is None:
                cursor[0] += size
            assert o + size <= nc.sbuf_usable_end, (name, o + size - nc.sbuf_usable_end)
            return nc.alloc_sbuf_tensor_at(name, shape, dt, offset=o, align_bytes=32)

        X = over("X", [P, KD, T])
        xnh0 = cursor[0]
        XNH = over("XNH", [P, KD, T], F32R)
        xnl0 = cursor[0]
        XNL = over("XNL", [P, KD, T], F32R)
        raw0 = cursor[0]
        RAW = over("RAW", [P, NRAW, UW])
        WH = over("WH", [P, NHL, UW], F32R)
        WL = over("WL", [P, NHL, UW], F32R)
        C = over("C", [P, CONST_N])
        PAR = over("PAR", [P, PAR_N])
        RGP = over("RGP", [P, 32])
        SQ = over("SQ", [P, 2, T])
        XF = over("XF", [P, 2, T])
        RS = over("RS", [P, T])
        QS = over("QS", [96, MH, NB])
        Q8 = over("Q8", [P, 2, NB])
        QL = over("QL", [P, NB, MH])
        QRB = over("QRB", [P, NB, 4, MH])
        C8 = over("C8", [NB, P])
        PT_SB = over("PT_SB", [1, NB * N_PAGES], I32)
        STAT = over("STAT", [P, 16])
        base = cursor[0]

        Z = over("Z", [P, 16, T])
        GXB = over("GXB", [P, RG, T + 8])
        qr0 = cursor[0]
        QR = over("QR", [P, 2, SEQ])
        SD = over("SD", [P, 2, NB * HD], at=qr0)
        UQ = over("UQ", [P, 2, 768])
        UK = over("UK", [P, 512])
        UKT = over("UKT", [64, MH, P])
        UV = over("UV", [P, 512])
        WG = over("WG", [P, 4, P])
        KT = over("KT", [P, 2, N_PAGES * P])
        RT = over("RT", [P, 2, 4 * P])
        gbase = cursor[0]
        PR = over("PR", [P, 1280])
        PTR = over("PTR", [P, 1280])
        V = over("V", [P, 4, 512])
        R = [over(f"R{i}", [P, T], at=gbase + 2080 * i) for i in range(6)]
        SM = over("SM", [P, 4, 512], at=gbase)
        VM = over("VM", [NB, RH, NB * HD], at=gbase + 8192)
        K8V8 = over("K8V8", [NB, 512], at=gbase + 16384)
        PD = over("PD", [P, NB * N_PAGES * MH], at=raw0)
        SMALL = over("SMALL", [P, 10, 64], at=raw0 + 4 * UW)
        VT = over("VT", [P, 4, 256], at=xnh0)
        KW = over("KW", [P, 4, 256], at=xnh0 + 6 * T * 4)
        QD = over("QD", [P, 2, 512], at=xnl0)
        SS = over("SS", [P, 4, 2 * HD], at=xnl0 + 6 * T * 4)
        QCs = [over(f"QC{i}", [96, 2, SEQ], at=xnh0 + i * 6 * T * 4) for i in range(2)]
        KCs = [over(f"KC{i}", [96, 2, SEQ], at=xnl0 + i * 6 * T * 4) for i in range(2)]
        cursor[0] = base
        HH = over("HH", [P, 12, T], F32R)
        HL = over("HL", [P, 12, T], F32R)
        GB = over("GB", [P, 2, T + 8])
        YC = over("YC", [P, 2, T])
        TH = over("TH", [P, 2, T])
        HF = over("HF", [P, 2, T])
        FOUT = over("FOUT", [P, NJ, 10])

        PS = [ctx.enter_context(nc.psum_tensor(f"PS{i}", [P, 2, 512], F32)) for i in range(4)]

        tables_in, pars_in, x_in, pt_in = sem("tables_in"), sem("pars_in"), sem("x_in"), sem("pt_in")
        small_in, sd_in = sem("small_in"), sem("sd_in")
        raw_full = [sem(f"raw_full{i}") for i in range(NRAW)]
        hi_split = [sem(f"hi_split{i}") for i in range(NHL)]
        lo_split = [sem(f"lo_split{i}") for i in range(NHL)]
        full_s = [sem(f"full{i}") for i in range(4)]
        emptied_s = [sem(f"emptied{i}") for i in range(4)]
        pages_in = [sem(f"pages_in{i}") for i in range(2)]
        pages_used = [sem(f"pages_used{i}") for i in range(2)]
        names = {"sq_ready": 21, "sq_used": SQ_MID[-1], "std_ready": 6, "xf_ready": 16, "xh_ready": 16, "xl_ready": 16,
                 "mid_used": 16, "roped": 6, "cq_normed": 3, "kr_roped": 1, "zeroed": 1,
                 "conv_done": 2, "rgp_half": 1, "lam_exp": 1, "lam_abs": 1, "q_ready": 2,
                 "tau_ready": 2, "a_ready": 2, "m_ready": 2, "g_ready": 2, "gl_sq": 2, "gl_arg": 2, "gl_tanh": 2,
                 "rg_done": 2, "kw_ready": 4, "qd_ready": 2, "vm_ready": 4, "gt_ready": 2, "gt_silu": 2, "ret_done": 2,
                 "mix_hi": 13, "mix_lo": 4, "qk_ready": 8, "kr_copied": 4, "nmax_ready": 8, "p_ready": 8,
                 "qs_ready": 4, "qrb_ready": 4, "m_all": 1, "sn_sub": 1, "pd_sub": 1, "pd_ready": 2, "rsum_ready": 1,
                 "gb_ready": NJ, "fout_ready": NJ, "conv_step": 3 * NJ, "yc_ready": NJ, "th_ready": NJ, "hf_ready": NJ,
                 "hh_ready": NJ, "hl_ready": NJ, "saved": 16 * 11, "ffn_free": 1}
        S = {n: (sem(n), k) for n, k in names.items()}
        settled, layers_saved = sem("settled"), sem("layers_saved")
        dve_chain, y_saved = sem("dve_chain"), [sem(f"y_saved{i}") for i in range(2)]

        def wait(e, name, l, c):
            s, per = S[name]
            e.wait_ge(s, l * per + c + (CREDIT if name == "hl_ready" else 0))

        def const(name, rows=slice(0, P), cols=None):
            o, w = CONST_AT[name]
            a, b = cols or (0, w)
            return C[rows, o + a:o + b]

        def par(name, a=0, b=None, rows=slice(0, P)):
            o, w = PAR_AT[name]
            return PAR[rows, o + a:o + (w if b is None else b)]

        def wait_full(e, l, name):
            i = TILE_AT[name]
            e.wait_ge(full_s[i % 4], l * NT4 + i // 4 + 1)

        def wait_emptied(e, l, name):
            i = TILE_AT[name]
            e.wait_ge(emptied_s[i % 4], l * NT4 + i // 4 + 1 + CREDIT)

        def wait_tile(e, l, name):
            i = TILE_AT[name]
            e.wait_ge(emptied_s[i % 4], l * NT4 + i // 4 + CREDIT)

        ps = lambda name: PS[TILE_AT[name] % 4]
        full = lambda name: full_s[TILE_AT[name] % 4]
        emptied = lambda name: emptied_s[TILE_AT[name] % 4]
        two = lambda ap: ap.rearrange("p (a n) -> p a n", a=2)
        psT = lambda name, r=slice(0, P): ps(name)[r, :, 0:HB]
        tables = lambda e: e.wait_ge(tables_in, 16)
        settle = lambda e: e.sem_inc(settled, 1)

        def rings_split(e, l, u):
            e.wait_ge(lo_split[u % NHL], l * (N_UNITS // NHL) + u // NHL + 1 + CREDIT)

        def before_layer(e, l):
            e.wait_ge(emptied_s[TILE_AT[f"dn1_{KD - 1}"] % 4], l * NT4 + CREDIT)

        block = ctx.enter_context(nc.Block())

        @block.sync
        def _(sp):
            sp.dma_start(C[:, :], constd).then_inc(tables_in, 16)
            for s in lo_split + emptied_s + pages_used:
                sp.sem_inc(s, CREDIT)
            for k in range(KD):
                sp.dma_start(X[:, k, :], xd[k]).then_inc(x_in, 16)
            sp.dma_start(PT_SB[:, :], ptd).then_inc(pt_in, 16)
            sp.wait_ge(pt_in, 16)

            def unit_wait(l, u):
                if u >= NRAW:
                    v = u - NRAW
                    sp.wait_ge(lo_split[v % NHL], l * (N_UNITS // NHL) + v // NHL + 1 + CREDIT)
                else:
                    sp.wait_ge(lo_split[u % NHL], l * (N_UNITS // NHL) + CREDIT)

            def one(l, u, width=UW):
                unit_wait(l, u)
                src = units[bass.ds(l * N_UNITS + u, 1), :, 0:width].rearrange("a p n -> p (a n)")
                sp.dma_start(RAW[:, u % NRAW, 0:width], src).then_inc(raw_full[u % NRAW], 16)

            def pages(l, phase, bp):
                before_layer(sp, l)
                settle(sp)
                sp.wait_ge(layers_saved, l + CREDIT)
                settle(sp)
                for s in range(2):
                    sp.wait_ge(pages_used[s], l * NB + phase * (NB // 2) + bp + CREDIT)
                    settle(sp)
                    for j0 in range(0, N_PAGES, 4):
                        at = bp * (2 * N_PAGES) + (s * N_PAGES + j0)
                        _, numbers = nc.values_load_multi_w_load_instructions(
                            PT_SB[0:1, bass.ds(at, 4)], engines=[mybir.EngineType.SP], min_val=0, max_val=N_PHYS - 1)
                        for j, page in enumerate(numbers, j0):
                            row = l * N_PHYS + page
                            sp.dma_start(KT[:, s, j * P:(j + 1) * P],
                                         (katd, kav)[phase][bass.ds(row, 1), :, :].rearrange("a p n -> p (a n)"))\
                                .then_inc(pages_in[s], 16)
                            if phase == 0:
                                g = 32 * (j % 4)
                                sp.dma_start(RT[g:g + 32, s, (j // 4) * P:(j // 4 + 1) * P],
                                             karp[bass.ds(row, 1), :, :].rearrange("a p n -> p (a n)"))\
                                    .then_inc(pages_in[s], 16)

            with sp.Fori(0, DEPTH) as l:
                for u in range(NRAW):
                    one(l, u)
                pages(l, 0, 0)
                for u in range(NRAW, N_IN_U + NRAW):
                    one(l, u, 256 if u == Z_KR else UW)
                with sp.Fori(0, NB // 2 - 1) as bp:
                    pages(l, 0, bp + 1)
                with sp.Fori(0, NB // 2) as bp:
                    pages(l, 1, bp)
                wait_full(sp, l, "dy")
                settle(sp)
                for u in range(N_IN_U + NRAW, U_UP[0]):
                    one(l, u)
                for u0, n, w in ((U_UP[0], 2 * HALVES[0][1], UW), (U_DN[0], 2 * KD, 6 * P),
                                 (U_UP[1], 2 * HALVES[1][1], UW), (U_DN[1], 2 * KD, 5 * P)):
                    with sp.Fori(0, n // NRAW) as it:
                        for j in range(NRAW):
                            v = u0 + j - NRAW
                            sp.wait_ge(lo_split[v % NHL], l * (N_UNITS // NHL) + it * (NRAW // NHL) + v // NHL + 1 + CREDIT)
                            row = l * N_UNITS + it * NRAW + (u0 + j)
                            sp.dma_start(RAW[:, (u0 + j) % NRAW, 0:w],
                                         units[bass.ds(row, 1), :, 0:w].rearrange("a p n -> p (a n)"))\
                                .then_inc(raw_full[(u0 + j) % NRAW], 16)

        @block.gpsimd
        def _(pool):
            pool.sem_inc(layers_saved, CREDIT)
            with pool.Fori(0, DEPTH) as l:
                tables(pool)
                before_layer(pool, l)
                pool.dma_start(PAR[:, :], pard[bass.ds(l, 1)].rearrange("a p n -> p (a n)")).then_inc(pars_in, 16)
                for dst, src in ((UQ[:, :, :], uqd), (UK[:, :], ukd), (UKT[:, :, :], uktd), (UV[:, :], uvd),
                                 (WG[:, :, :], wgd)):
                    s = src[bass.ds(l, 1)]
                    s = s.rearrange("a p k n -> p (a k) n") if len(dst.shape) == 3 else s.rearrange("a p n -> p (a n)")
                    pool.dma_start(dst, s).then_inc(small_in, 16)
                pool.dma_start(SD[:, :, :], s0d[bass.ds(l, 1)].rearrange("a p k n -> p (a k) n")).then_inc(sd_in, 16)
                saved = S["saved"][0]
                pool.dma_start(rgc0_o[bass.ds(l, 1)], cpd[bass.ds(l, 1)]).then_inc(saved, 16)
                pool.dma_start(ffc0_o[bass.ds(l, 1)], fpd[bass.ds(l, 1)]).then_inc(saved, 16)
                sl = lambda o: o[bass.ds(l, 1)].rearrange("a p n -> p (a n)")
                wait(pool, "cq_normed", l, 1)
                pool.dma_start(sl(lat_o), Z[:, Z_CKV, :]).then_inc(saved, 16)
                wait(pool, "kr_roped", l, 1)
                pool.dma_start(sl(rope_o), Z[0:32, Z_KR, :]).then_inc(saved, 16)
                wait_emptied(pool, l, "in10")
                pool.dma_start(gx_o[bass.ds(2 * l, 1)].rearrange("a p n -> p (a n)"), GXB[:, 0, SEQ:T + 3]).then_inc(saved, 16)
                wait_emptied(pool, l, "in11")
                pool.dma_start(gx_o[bass.ds(2 * l + 1, 1)].rearrange("a p n -> p (a n)"), GXB[:, 1, SEQ:T + 3]).then_inc(saved, 16)
                wait(pool, "rg_done", l, 1)
                pool.dma_start(hr_o[bass.ds(2 * l, 1)].rearrange("a p n -> p (a n)"), Z[:, 10, SEQ - 1:T]).then_inc(saved, 16)
                wait(pool, "rg_done", l, 2)
                pool.dma_start(hr_o[bass.ds(2 * l + 1, 1)].rearrange("a p n -> p (a n)"), Z[:, 11, SEQ - 1:T]).then_inc(saved, 16)
                wait_emptied(pool, l, "kv")
                pool.dma_start(sl(pret_o), SS[:, 3, :]).then_inc(saved, 16)
                wait_emptied(pool, l, "du")
                settle(pool)
                pool.dma_start(sret_o[bass.ds(l, 1)].rearrange("a p k n -> p (a k) n"), SD[:, :, :]).then_inc(saved, 16)
                wait(pool, "fout_ready", l, NJ)
                pool.dma_start(ff_o[bass.ds(l, 1)].rearrange("a p k n -> p (a k) n"), FOUT[:, :, :]).then_inc(saved, 16)
                wait(pool, "saved", l, 16 * 11)
                pool.sem_inc(layers_saved, 1)
            for k in range(KD):
                wait(pool, "xf_ready", DEPTH, k + 1)
                pool.dma_start(y_o[k], XF[:, k % 2, :]).then_inc(y_saved[k % 2], 16)
            pool.wait_ge(y_saved[0], 16 * KD // 2)
            pool.wait_ge(y_saved[1], 16 * KD // 2)

        @block.scalar
        def _(act):
            def hi(l, u, it=None, tile=None, mid=None):
                a = l * (N_UNITS // NRAW) + u // NRAW + 1
                if it is not None:
                    a = a + it * (1 if u < U_DN[0] or U_UP[1] <= u < U_DN[1] else 2)
                act.wait_ge(raw_full[u % NRAW], a * 16)
                if mid is not None:
                    b = l * S["mid_used"][1] + mid
                    act.wait_ge(S["mid_used"][0], b if it is None else b + it * 4)
                elif tile is not None:
                    b = l * NT4 + TILE_AT[tile] // 4 + 1
                    act.wait_ge(full_s[TILE_AT[tile] % 4], b if it is None else b + it)
                tables(act)
                act.activation(WH[:, u % NHL, :], RAW[:, u % NRAW, :], ACT.Copy).then_inc(hi_split[u % NHL], 1)

            def hi_down(l, hf, x, it=None):
                m = x // 2
                u = U_DN[hf] + x + 2
                if x % 2 == 0:
                    hi(l, u, it, mid=8 * hf + m + 1)
                else:
                    hi(l, u, it, tile=f"dn{hf}_{m}")

            def square_free(l, q):
                if q >= 2:
                    t, k, n = SQ_USES[q - 2]
                    if k < n - 1:
                        wait(act, "sq_used", l, SQ_MID[q - 1])
                    else:
                        wait_full(act, l, t)

            def squares(l, q0, aps, before):
                for k, ap in enumerate(aps):
                    before(k)
                    q = q0 + k
                    square_free(l, q)
                    act.activation(SQ[:, q % 2, :], ap, ACT.Square).then_inc(S["sq_ready"][0], 1)

            def root(l, name, n):
                wait_emptied(act, l, name)
                act.activation(RS[:, :], RS[:, :], ACT.Sqrt).then_inc(S["std_ready"][0], 1)

            def heads_of_norm(l, c0):
                for k in range(KD):
                    wait(act, "xf_ready", l, c0 + k + 1)
                    act.activation(XNH[:, k, :], XF[:, k % 2, :], ACT.Copy).then_inc(S["xh_ready"][0], 1)

            def evac(l, name, dst, src, **kw):
                wait_full(act, l, name)
                act.activation(dst, src, kw.pop("func", ACT.Copy), **kw).then_inc(emptied(name), 1)

            act.wait_ge(x_in, 16 * KD)
            with act.Fori(0, DEPTH) as l:
                before_layer(act, l)
                hi(l, 0)
                before_layer(act, l)
                hi(l, 1)
                squares(l, 0, [X[:, k, :] for k in range(KD)], lambda k: before_layer(act, l))
                root(l, "n1", 0)
                heads_of_norm(l, 0)
                for u in range(N_IN_U):
                    if u in Z_GX:
                        dst = two(GXB[:, u - 10, 3:T + 3])
                    elif u == Z_KR:
                        dst = two(Z[0:32, u, :])
                    else:
                        dst = two(Z[:, u, :])
                    r = slice(0, 32) if u == Z_KR else slice(0, P)
                    evac(l, f"in{u}", dst, psT(f"in{u}", r), scale=0.125 if u in Z_RK else 1.0)
                    hi(l, u + 2, tile=f"in{u}")
                    if u == 2:
                        squares(l, 8, [Z[:, 0, :]], lambda k: wait_emptied(act, l, "in0"))
                        squares(l, 9, [Z[:, 1, :], Z[:, 2, :]], lambda k: wait_emptied(act, l, f"in{k + 1}"))
                    if u == 5:
                        root(l, "nckv", 1)
                    if u == 7:
                        root(l, "ncq", 2)
                wait_full(act, l, "q8")
                for i in range(2):
                    act.activation(QS[0:64, :, :].rearrange("p (a i) b -> p a i b", i=2)[:, :, i, :],
                                   ps("q8")[64 * i:64 * i + 64, 0, 0:4 * NB].rearrange("p (a b) -> p a b", b=NB), ACT.Copy)
                act.activation(Q8[:, :, :], ps("q8")[:, 0, 4 * NB:6 * NB].rearrange("p (a b) -> p a b", b=NB), ACT.Copy)\
                    .then_inc(emptied("q8"), 1)
                for i in range(4):
                    wait(act, "qs_ready", l, 4)
                    tables(act)
                    act.activation(QRB[32 * i:32 * i + 32, :, i, :], QS[64:96, :, :].rearrange("p h b -> p b h"),
                                   ACT.Copy).then_inc(S["qrb_ready"][0], 1)
                evac(l, "ql", QL[:, :, :], ps("ql")[:, 0, 0:64].rearrange("p (h b) -> p b h", h=MH))
                wait(act, "lam_abs", l, 1)
                act.activation(RGP[:, 6:8], RGP[:, 4:6], ACT.Exp, scale=-1.0).then_inc(S["lam_exp"][0], 1)
                wait(act, "rgp_half", l, 1)
                for c in range(RG):
                    tr, ti, q, tau, a, g = (R[i][:, :] for i in range(6))
                    if c:
                        wait(act, "rg_done", l, c)
                    evac(l, f"g{c}r", two(tr), psT(f"g{c}r"), func=ACT.Tanh, scale=0.5, bias=RGP[:, c:c + 1])
                    evac(l, f"g{c}i", two(ti), psT(f"g{c}i"), func=ACT.Tanh, scale=0.5, bias=RGP[:, 2 + c:3 + c])
                    wait(act, "q_ready", l, c + 1)
                    act.activation(tau, q, ACT.Tanh).then_inc(S["tau_ready"][0], 1)
                    act.activation(a, q, ACT.Exp, scale=-1.0).then_inc(S["a_ready"][0], 1)
                    wait_emptied(act, l, f"in{12 + c}")
                    act.activation(tr, Z[:, 12 + c, :], ACT.Square).then_inc(S["gl_sq"][0], 1)
                    wait(act, "gl_arg", l, c + 1)
                    act.activation(tr, tr, ACT.Tanh, scale=G_C2).then_inc(S["gl_tanh"][0], 1)
                    wait(act, "m_ready", l, c + 1)
                    act.activation(g, g, ACT.Sqrt).then_inc(S["g_ready"][0], 1)
                for i in range(2):
                    wait_full(act, l, f"rt{i}")
                    wait(act, "kw_ready", l, 2 * i + 2)
                    act.activation(VT[:, 2 * i:2 * i + 2, :], ps(f"rt{i}")[:, :, 0:256], ACT.Copy)\
                        .then_inc(emptied(f"rt{i}"), 1)
                wait_full(act, l, "ro")
                for c in range(2):
                    i = act.activation(Z[:, 8 + c, 0:SEQ], ps("ro")[:, c, :], ACT.Copy)
                i.then_inc(emptied("ro"), 1)
                wait_full(act, l, "dk")
                act.activation(C8[:, :], ps("dk")[0:NB, 1, 0:P], ACT.Copy)
                act.activation(K8V8[:, :], ps("dk")[0:NB, 0, :], ACT.Copy).then_inc(emptied("dk"), 1)
                wait_full(act, l, "do")
                for i in range(2):
                    r = slice(64 * i, 64 * i + 64)
                    ins = act.activation(Z[r, 8:10, SEQ:T], ps("do")[r, i, 0:2 * NB].rearrange("p (c b) -> p c b", c=2),
                                         ACT.Copy)
                ins.then_inc(emptied("do"), 1)
                for c in range(2):
                    wait_emptied(act, l, f"in{14 + c}")
                    wait(act, "rg_done", l, 2)
                    act.activation(XF[:, c, :], Z[:, 14 + c, :], ACT.Tanh, scale=0.5).then_inc(S["gt_ready"][0], 1)
                for c in range(2):
                    wait_emptied(act, l, f"gm{c}")
                    square_free(l, 11 + c)
                    act.activation(SQ[:, (11 + c) % 2, :], Z[:, 8 + c, :], ACT.Square).then_inc(S["sq_ready"][0], 1)
                for c in range(2):
                    root(l, f"gv{c}", 3)
                for c in range(2):
                    wait(act, "saved", l, 16 * 10)
                    evac(l, f"qr{c}", QR[:, c, :], ps(f"qr{c}")[:, 0, :])
                for i, name in enumerate(("v01", "v23")):
                    wait(act, "ret_done", l, 2)
                    evac(l, name, V[:, 2 * i:2 * i + 2, :], ps(name)[:, :, :])
                for i in range(4):
                    wait(act, "kr_roped", l, 1)
                    wait_full(act, l, "v23")
                    act.activation(KCs[i // 2][64:96, i % 2, :], Z[0:32, Z_KR, 0:SEQ], ACT.Copy).then_inc(S["kr_copied"][0], 1)
                for h in range(MH + 1):
                    if h < MH:
                        p, s = h // 2, (h // 2) % 2
                        if h % 2 == 0:
                            if p >= 2:
                                wait_full(act, l, f"sB{2 * p - 3}")
                            wait_full(act, l, f"q{p}")
                            tables(act)
                            act.activation(QCs[s][0:64, 0, :], ps(f"q{p}")[0:64, 0, :], ACT.Copy)
                            act.activation(QCs[s][0:64, 1, :], ps(f"q{p}")[64:P, 0, :], ACT.Copy).then_inc(emptied(f"q{p}"), 1)
                            wait_full(act, l, f"k{p}")
                            tables(act)
                            act.activation(KCs[s][0:64, 0, :], ps(f"k{p}")[0:64, 0, :], ACT.Copy)
                            act.activation(KCs[s][0:64, 1, :], ps(f"k{p}")[64:P, 0, :], ACT.Copy).then_inc(emptied(f"k{p}"), 1)
                        wait(act, "nmax_ready", l, h + 1)
                        if h:
                            wait_full(act, l, f"tB{h - 1}")
                        for q in range(4):
                            o = 128 * (q * (q + 1) // 2)
                            n = f"s{'AB'[q // 2]}{h}"
                            i = act.activation(PR[:, o:o + 128 * (q + 1)], ps(n)[:, q % 2, 0:128 * (q + 1)], ACT.Exp,
                                               scale=SCALE, bias=STAT[:, q:q + 1], accum_out=STAT[:, 8 + q:9 + q])
                            if q % 2:
                                i.then_inc(emptied(n), 1)
                    if h:
                        g = h - 1
                        if g:
                            wait_full(act, l, f"o{g - 1}")
                        wait_full(act, l, f"tA{g}")
                        act.activation(PTR[:, 0:512], ps(f"tA{g}")[:, 0, :], ACT.Copy)
                        act.activation(PTR[:, 512:896], ps(f"tA{g}")[:, 1, 0:384], ACT.Copy).then_inc(emptied(f"tA{g}"), 1)
                        wait_full(act, l, f"o{g}")
                        r = slice(64 * (g % 2), 64 * (g % 2) + 64)
                        act.activation(XNH[r, 2 + g // 2, 0:SEQ], ps(f"o{g}")[r, 0, :], ACT.Copy).then_inc(S["mix_hi"][0], 1)
                    if "db" in DECODE_TILES[h]:
                        wait(act, "pd_sub", l, 1)
                        act.activation(PD[:, :], PD[:, :], ACT.Exp, scale=SCALE).then_inc(S["pd_ready"][0], 1)
                        act.activation(SMALL[0:NB, 1, :], SMALL[0:NB, 1, :], ACT.Exp, scale=SCALE).then_inc(S["pd_ready"][0], 1)
                    if "dy" in DECODE_TILES[h]:
                        wait_full(act, l, "dy")
                        act.activation(XNH[:, 2:6, SEQ:T], ps("dy")[:, 0, 0:4 * NB].rearrange("p (c b) -> p c b", c=4),
                                       ACT.Copy).then_inc(S["mix_hi"][0], 1)
                for i, (src, dst) in enumerate(((8, 0), (9, 1), (12, 6), (13, 7))):
                    wait(act, "ret_done", l, 2)
                    act.activation(XNH[:, dst, :], Z[:, src, :], ACT.Copy, scale=0.5)\
                        .then_inc(S["mix_hi"][0], 1)
                with act.Fori(0, KD // 4) as it:
                    for j in range(4):
                        hi(l, U_OUT + j + 2, it, tile=f"wo{j}")
                squares(l, 13, [X[:, k, :] for k in range(KD)], lambda k: wait_emptied(act, l, f"wo{KD - 1}"))
                root(l, "n2", 5)
                heads_of_norm(l, KD)
                wait(act, "saved", l, 16 * 10)
                act.activation(GB[:, 0, 0:2], const("zero", cols=(0, 2)), ACT.Copy)
                act.activation(GB[:, 1, 0:2], const("zero", cols=(0, 2)), ACT.Copy).then_inc(S["ffn_free"][0], 1)
                for hf, (j0, n) in enumerate(HALVES):
                    t0 = TILE_AT[f"up{hf}_0"]
                    with act.Fori(0, n // 2) as it:
                        for jj in range(2):
                            gi, vi = t0 + 2 * jj, t0 + 2 * jj + 1
                            c = it * 2 + (j0 + jj)
                            col = it * 2 + (PAR_AT["fcw"][0] + j0 + jj)
                            g_full = l * NT4 + it + (gi // 4 + 1)
                            wait(act, "hl_ready", l, c)
                            act.wait_ge(full_s[gi % 4], g_full)
                            tables(act)
                            act.activation(two(GB[:, jj, 2:T + 2]), PS[gi % 4][:, :, 0:HB], ACT.Copy).then_inc(S["gb_ready"][0], 1)
                            act.activation(two(YC[:, jj, :]), PS[gi % 4][:, :, 0:HB], ACT.Identity,
                                           scale=PAR[:, bass.ds(col + 2 * NJ, 1)], bias=PAR[:, bass.ds(col + 3 * NJ, 1)])\
                                .then_inc(emptied_s[gi % 4], 1)
                            hi(l, U_UP[hf] + 2 * jj + 2, it, tile=f"up{hf}_{2 * jj}")
                            wait(act, "yc_ready", l, c + 1)
                            act.activation(TH[:, jj, :], YC[:, jj, :], ACT.Tanh, scale=0.5).then_inc(S["th_ready"][0], 1)
                            hi(l, U_UP[hf] + 2 * jj + 3, it, tile=f"up{hf}_{2 * jj + 1}")
                            act.wait_ge(emptied_s[vi % 4], l * NT4 + it + (vi // 4 + 1 + CREDIT))
                            tables(act)
                            act.activation(HH[:, bass.ds(it * 2 + jj, 1), :], HF[:, jj:jj + 1, :], ACT.Copy)\
                                .then_inc(S["hh_ready"][0], 1)
                    if hf == 0:
                        with act.Fori(0, 2) as it:
                            for j in range(8):
                                hi_down(l, hf, j, it)
                    else:
                        for j in range(14):
                            hi_down(l, hf, j)
            squares(DEPTH, 0, [X[:, k, :] for k in range(KD)], lambda k: before_layer(act, DEPTH))
            root(DEPTH, "n1", 0)

        @block.vector
        def _(dve):
            V_ = nc.vector
            links = [0]
            D_LINKS = DVE_LINKS
            lay = [0]

            def link(ins):
                links[0] += 1
                ins.then_inc(dve_chain, 1)
                dve.wait_ge(dve_chain, lay[0] * D_LINKS + links[0])

            def lo(l, u, it=None, per=0):
                a = l * (N_UNITS // NHL) + u // NHL + 1
                if it is not None:
                    a = a + it * (per // NHL)
                dve.wait_ge(hi_split[u % NHL], a)
                V_.tensor_tensor(WL[:, u % NHL, :], RAW[:, u % NRAW, :], WH[:, u % NHL, :].bitcast(F32), ALU.subtract)\
                    .then_inc(lo_split[u % NHL], 1)

            def variance(l, name, n):
                wait_full(dve, l, name)
                V_.tensor_scalar(two(RS[:, :]), psT(name), 1.0 / n, EPS, ALU.mult, ALU.add).then_inc(emptied(name), 1)

            def norm(l, name, std_no, c0, wname, split=True):
                variance(l, name, D_MODEL)
                wait(dve, "std_ready", l, std_no)
                link(V_.reciprocal(RS[:, :], RS[:, :]))

                def low(k):
                    wait(dve, "xh_ready", l, c0 + k + 1)
                    V_.tensor_tensor(XNL[:, k, :], XF[:, k % 2, :], XNH[:, k, :].bitcast(F32), ALU.subtract)\
                        .then_inc(S["xl_ready"][0], 1)

                for k in range(KD):
                    if k >= 2:
                        if split:
                            wait(dve, "xl_ready", l, c0 + k - 1)
                        else:
                            dve.wait_ge(y_saved[k % 2], 16 * (k // 2))
                    V_.scalar_tensor_tensor(XF[:, k % 2, :], X[:, k, :], par(wname, k, k + 1), RS[:, :],
                                            ALU.mult, ALU.mult).then_inc(S["xf_ready"][0], 1)
                    if split and k:
                        low(k - 1)
                if split:
                    low(KD - 1)

            def rope(l, name, z, rows, cs, sn, former, done):
                wait_full(dve, l, name)
                wait(dve, former[0], l, former[1])
                V_.tensor_tensor(two(XF[rows, 0, :]), psT(name, rows), two(const(sn, rows)), ALU.mult).then_inc(emptied(name), 1)
                link(V_.tensor_tensor(z, z, const(cs, rows), ALU.mult))
                wait_emptied(dve, l, name)
                V_.tensor_tensor(z, z, XF[rows, 0, :], ALU.add).then_inc(S[done][0], 1)

            V_.memset(QRB[:, :, :, :], 0.0)
            V_.memset(STAT[:, :], 0.0)
            dve.sem_inc(S["hl_ready"][0], 1 + CREDIT)
            dve.wait_ge(x_in, 16 * KD)
            with dve.Fori(0, DEPTH) as l:
                lay[0] = l
                links[0] = 0
                dve.wait_ge(pars_in, l * 16 + 16)
                tables(dve)
                lo(l, 0)
                lo(l, 1)
                norm(l, "n1", 1, 0, "n1")
                V_.memset(GXB[:, :, 0:3], 0.0).then_inc(S["zeroed"][0], 1)
                V_.tensor_scalar(RGP[:, 0:4], par("ba", 0, 4), 0.5, None, ALU.mult).then_inc(S["rgp_half"][0], 1)
                link(V_.tensor_scalar(RGP[:, 8:10], par("lam"), -1.0, None, ALU.mult))
                V_.tensor_tensor(RGP[:, 4:6], RGP[:, 8:10], par("lam"), ALU.max).then_inc(S["lam_abs"][0], 1)
                for u in range(2, N_IN_U + 2):
                    lo(l, u)
                    if u == 6:
                        wait(dve, "xf_ready", l, KD)
                        variance(l, "nckv", KVR)
                    if u == 8:
                        wait(dve, "std_ready", l, 2)
                        link(V_.reciprocal(RS[:, :], RS[:, :]))
                        V_.scalar_tensor_tensor(Z[:, 0, :], Z[:, 0, :], par("kn"), RS[:, :], ALU.mult, ALU.mult)\
                            .then_inc(S["cq_normed"][0], 1)
                        wait(dve, "cq_normed", l, 1)
                        variance(l, "ncq", QR_)
                    if u == 10:
                        wait(dve, "std_ready", l, 3)
                        link(V_.reciprocal(RS[:, :], RS[:, :]))
                        for k in range(2):
                            V_.scalar_tensor_tensor(Z[:, 1 + k, :], Z[:, 1 + k, :], par("qn", k, k + 1), RS[:, :],
                                                    ALU.mult, ALU.mult).then_inc(S["cq_normed"][0], 1)
                rope(l, "pkr", Z[0:32, Z_KR, :], slice(0, 32), "cosm", "sinm", ("xl_ready", KD), "kr_roped")
                for i, z in enumerate((3, 5, 6, 7)):
                    rope(l, f"pz{i}", Z[:, z, :], slice(0, P), "cosr", "sinr", ("roped", i) if i else ("kr_roped", 1), "roped")
                cs = lambda n: const(n, cols=(SEQ, T)).rearrange("p (a b) -> p a b", a=1).broadcast_to([P, 2, NB])
                pq = ps("pq8")[:, 0, 0:2 * NB].rearrange("p (a b) -> p a b", b=NB)
                wait_full(dve, l, "pq8")
                V_.tensor_tensor(pq, pq, cs("sinm"), ALU.mult)
                link(V_.tensor_tensor(Q8[:, :, :], Q8[:, :, :], cs("cosm"), ALU.mult))
                V_.tensor_tensor(Q8[:, :, :], Q8[:, :, :], pq, ALU.add).then_inc(emptied("pq8"), 1)
                wait_emptied(dve, l, "pq8")
                for i in range(4):
                    V_.tensor_copy(QS[64:96, :, :].rearrange("p (a i) b -> p a i b", i=4)[:, :, i, :],
                                   Q8[32 * i:32 * i + 32, :, :]).then_inc(S["qs_ready"][0], 1)
                SN, PN, M1, MB, RSUM, RD, OL = (SMALL[:, i, :] for i in range(7))

                def page_scores(b):
                    wait_full(dve, l, f"ds{b}")
                    dve.sem_inc(pages_used[b % 2], 1)
                    rings_split(dve, l, N_IN_U)
                    rings_split(dve, l, N_IN_U + 1)
                    n = N_PAGES * MH
                    V_.tensor_copy(PD[:, n * b:n * b + n], ps(f"ds{b}")[:, 0, 0:n])
                    V_.tensor_reduce(M1[:, MH * b:MH * b + MH], ps(f"ds{b}")[:, 0, 0:n].rearrange("p (j h) -> p h j", h=MH),
                                     AX, ALU.max).then_inc(emptied(f"ds{b}"), 1)

                s2, e_, pp = RGP[:, 10:12], RGP[:, 6:8], RGP[:, 12:14]
                s_ = RGP[:, 14:16]
                wait(dve, "lam_exp", l, 1)
                link(V_.tensor_scalar(s_, e_, 2.0, None, ALU.add))
                link(V_.reciprocal(s_, s_))
                link(V_.tensor_tensor(s_, s_, e_, ALU.mult))
                link(V_.tensor_tensor(s2, s_, s_, ALU.mult))
                link(V_.tensor_scalar(pp, s2, 1.0 / 21, None, ALU.mult))
                for k in range(9, 0, -1):
                    link(V_.scalar_tensor_tensor(pp, pp, 1.0 / (2 * k + 1), s2, ALU.add, ALU.mult))
                link(V_.scalar_tensor_tensor(pp, pp, 1.0, s_, ALU.add, ALU.mult))
                link(V_.tensor_scalar(RGP[:, 8:10], RGP[:, 8:10], 0.0, 4.0, ALU.max, ALU.mult))
                link(V_.scalar_tensor_tensor(RGP[:, 16:18], pp, 8.0, RGP[:, 8:10], ALU.mult, ALU.add))
                for c in range(RG):
                    xc = Z[:, 10 + c, :]
                    w = lambda k: par("rcw", 4 * c + k, 4 * c + k + 1)
                    wait_emptied(dve, l, f"in{10 + c}")
                    wait(dve, "zeroed", l, 1)
                    link(V_.tensor_scalar(xc, GXB[:, c, 3:T + 3], w(3), par("rcb", c, c + 1), ALU.mult, ALU.add))
                    for k in range(RGC - 1):
                        link(V_.scalar_tensor_tensor(xc[:, 0:SEQ], GXB[:, c, k:k + SEQ], w(k), xc[:, 0:SEQ], ALU.mult, ALU.add))
                        i = V_.scalar_tensor_tensor(xc[:, SEQ:T], par("cbuf", 24 * c + 8 * k, 24 * c + 8 * k + 8), w(k),
                                                    xc[:, SEQ:T], ALU.mult, ALU.add)
                        if k < RGC - 2:
                            link(i)
                        else:
                            i.then_inc(S["conv_done"][0], 1)
                page_scores(0)
                page_scores(1)
                wait(dve, "conv_done", l, 2)
                for c in range(RG):
                    tr, ti, q, tau, a, g = (R[i][:, :] for i in range(6))
                    sp4, gg, xc = RGP[:, 16 + c:17 + c], Z[:, 12 + c, :], Z[:, 10 + c, :]
                    wait_emptied(dve, l, f"g{c}r")
                    V_.tensor_scalar(q, tr, sp4, sp4, ALU.mult, ALU.add).then_inc(S["q_ready"][0], 1)
                    wait(dve, "tau_ready", l, c + 1)
                    link(V_.tensor_scalar(g, tau, 1.0, None, ALU.add))
                    link(V_.reciprocal(g, g))
                    V_.scalar_tensor_tensor(g, tau, 2.0, g, ALU.mult, ALU.mult).then_inc(S["m_ready"][0], 1)
                    wait_emptied(dve, l, f"g{c}i")
                    link(V_.scalar_tensor_tensor(ti, ti, 1.0, xc, ALU.add, ALU.mult))
                    wait(dve, "gl_sq", l, c + 1)
                    link(V_.tensor_scalar(tr, tr, G_C1, 1.0, ALU.mult, ALU.add))
                    V_.tensor_tensor(tr, tr, gg, ALU.mult).then_inc(S["gl_arg"][0], 1)
                    wait(dve, "g_ready", l, c + 1)
                    link(V_.scalar_tensor_tensor(ti, ti, 0.5, g, ALU.mult, ALU.mult))
                    wait(dve, "a_ready", l, c + 1)
                    link(V_.tensor_tensor_scan(xc[:, 0:SEQ], a[:, 0:SEQ], ti[:, 0:SEQ], 0.0, ALU.mult, ALU.add))
                    link(V_.tensor_tensor(q[:, 0:NB], a[:, SEQ:T], par("h0", 8 * c, 8 * c + 8), ALU.mult))
                    link(V_.tensor_tensor(xc[:, SEQ:T], q[:, 0:NB], ti[:, SEQ:T], ALU.add))
                    wait(dve, "gl_tanh", l, c + 1)
                    link(V_.scalar_tensor_tensor(gg, tr, 1.0, gg, ALU.add, ALU.mult))
                    V_.tensor_tensor(gg, gg, xc, ALU.mult).then_inc(S["rg_done"][0], 1)
                wait(dve, "rg_done", l, 2)
                for c in range(2):
                    gq = const("gq", cols=(P * c, P * c + P)).rearrange("p (a t) -> p a t", a=1).broadcast_to([P, 4, P])
                    wait(dve, "roped", l, 4)
                    V_.tensor_tensor(QD[:, c, :].rearrange("p (a t) -> p a t", a=4),
                                     Z[:, (3, 5)[c], 0:SEQ].rearrange("p (a t) -> p a t", a=4), gq, ALU.mult)\
                        .then_inc(S["qd_ready"][0], 1)
                for n in range(4):
                    wait_full(dve, l, f"rt{n // 2}")
                    V_.tensor_tensor(KW[:, n, :], ps(f"rt{n // 2}")[:, n % 2, 256:512], const("wk"), ALU.mult)\
                        .then_inc(S["kw_ready"][0], 1)
                for n in range(4):
                    t = f"rs{n // 2}"
                    wait_full(dve, l, t)
                    i = V_.tensor_tensor(two(SM[:, n, :]), ps(t)[:, :, 256 * (n % 2):256 * (n % 2) + 256],
                                         two(const("decay")), ALU.mult)
                    if n % 2:
                        i.then_inc(emptied(t), 1)
                wait_full(dve, l, "kv")
                link(V_.tensor_copy(SS[:, 0, :], ps("kv")[:, 0, 0:P]))
                for n in range(1, 4):
                    for c in range(2):
                        i = V_.scalar_tensor_tensor(SS[:, n, HD * c:HD * c + HD], SS[:, n - 1, HD * c:HD * c + HD],
                                                    const("gam", cols=(c, c + 1)),
                                                    ps("kv")[:, 0, P * n + HD * c:P * n + HD * c + HD], ALU.mult, ALU.add)
                        if (n, c) == (3, 1):
                            i.then_inc(emptied("kv"), 1)
                        elif c:
                            link(i)
                page_scores(2)
                page_scores(3)
                wait_emptied(dve, l, "dk")
                for h in range(RH):
                    v8 = K8V8[:, 256 + HD * h:256 + HD * h + HD].rearrange("p (a e) -> p a e", a=1).broadcast_to([NB, NB, HD])
                    V_.tensor_tensor(VM[:, h, :].rearrange("p (b e) -> p b e", b=NB), v8,
                                     const("bmask", slice(0, NB)).rearrange("p (b e) -> p b e", b=NB), ALU.mult)\
                        .then_inc(S["vm_ready"][0], 1)
                wait_full(dve, l, "du")
                dve.wait_ge(sd_in, l * 16 + 16)
                for c in range(2):
                    i = V_.scalar_tensor_tensor(SD[:, c, :], SD[:, c, :], const("gam", cols=(2 + c, 3 + c)),
                                                ps("du")[:, c, :], ALU.mult, ALU.add)
                i.then_inc(emptied("du"), 1)
                for c in range(2):
                    wait_full(dve, l, f"gm{c}")
                    V_.tensor_tensor(two(Z[:, 8 + c, :]), two(Z[:, 8 + c, :]), psT(f"gm{c}"), ALU.subtract).then_inc(emptied(f"gm{c}"), 1)
                page_scores(4)
                page_scores(5)
                for c in range(2):
                    wait(dve, "gt_ready", l, c + 1)
                    V_.scalar_tensor_tensor(Z[:, 14 + c, :], XF[:, c, :], 1.0, Z[:, 14 + c, :], ALU.add, ALU.mult)\
                        .then_inc(S["gt_silu"][0], 1)
                for c in range(2):
                    variance(l, f"gv{c}", 1.0)
                    wait(dve, "std_ready", l, 4 + c)
                    link(V_.reciprocal(RS[:, :], RS[:, :]))
                    link(V_.scalar_tensor_tensor(Z[:, 8 + c, :], Z[:, 8 + c, :], par("gn", c, c + 1), RS[:, :], ALU.mult, ALU.mult))
                    V_.tensor_tensor(Z[:, 8 + c, :], Z[:, 8 + c, :], Z[:, 14 + c, :], ALU.mult).then_inc(S["ret_done"][0], 1)
                wait(dve, "ret_done", l, 2)
                for c in range(2):
                    wait_emptied(dve, l, f"qr{c}")
                    wait_full(dve, l, f"pqr{c}")
                    wait(dve, *(("roped", l, 5) if c else ("gt_silu", l, 2)))
                    V_.tensor_tensor(XF[:, 0, 0:SEQ], ps(f"pqr{c}")[:, 0, :], const("sinm", cols=(0, SEQ)), ALU.mult)\
                        .then_inc(emptied(f"pqr{c}"), 1)
                    link(V_.tensor_tensor(QR[:, c, :], QR[:, c, :], const("cosm", cols=(0, SEQ)), ALU.mult))
                    wait_emptied(dve, l, f"pqr{c}")
                    V_.tensor_tensor(QR[:, c, :], QR[:, c, :], XF[:, 0, 0:SEQ], ALU.add).then_inc(S["roped"][0], 1)
                wait(dve, "roped", l, 6)
                for h in range(MH + 1):
                    if h < MH:
                        p, s = h // 2, (h // 2) % 2
                        if h % 2 == 0:
                            for i in range(2):
                                wait_full(dve, l, f"q{p}")
                                r = 32 * ((2 * p + i) % 4)
                                V_.tensor_copy(QCs[s][64:96, i, :], QR[r:r + 32, p // 2, :]).then_inc(S["qk_ready"][0], 1)
                        for q in range(4):
                            n = f"s{'AB'[q // 2]}{h}"
                            if q % 2 == 0:
                                wait_full(dve, l, n)
                            dg = ps(n)[:, q % 2, 128 * q:128 * q + 128]
                            i = V_.tensor_tensor(dg, dg, const("causal"), ALU.add)
                        link(i)
                        for q in range(4):
                            n = f"s{'AB'[q // 2]}{h}"
                            i = V_.tensor_reduce(STAT[:, 4 + q:5 + q], ps(n)[:, q % 2, 0:128 * (q + 1)], AX, ALU.max)
                        link(i)
                        V_.tensor_scalar(STAT[:, 0:4], STAT[:, 4:8], -SCALE, None, ALU.mult).then_inc(S["nmax_ready"][0], 1)
                    if h:
                        g = h - 1
                        if g:
                            wait_full(dve, l, f"o{g - 1}")
                        wait_full(dve, l, f"tB{g}")
                        V_.tensor_copy(PTR[:, 896:1152], ps(f"tB{g}")[:, 0, 0:256])
                        V_.tensor_copy(PTR[:, 1152:1280], ps(f"tB{g}")[:, 1, 0:128]).then_inc(emptied(f"tB{g}"), 1)
                    if h < MH:
                        wait_emptied(dve, l, f"sA{h}")
                        wait_emptied(dve, l, f"sB{h}")
                        link(V_.reciprocal(STAT[:, 12:16], STAT[:, 8:12]))
                        for q in range(4):
                            o = 128 * (q * (q + 1) // 2)
                            i = V_.tensor_scalar(PR[:, o:o + 128 * (q + 1)], PR[:, o:o + 128 * (q + 1)],
                                                 STAT[:, 12 + q:13 + q], None, ALU.mult)
                        i.then_inc(S["p_ready"][0], 1)
                    if h:
                        g = h - 1
                        r = slice(64 * (g % 2), 64 * (g % 2) + 64)
                        wait(dve, "mix_hi", l, g + 1)
                        V_.tensor_tensor(XNL[r, 2 + g // 2, 0:SEQ], ps(f"o{g}")[r, 0, :], XNH[r, 2 + g // 2, 0:SEQ].bitcast(F32),
                                         ALU.subtract).then_inc(emptied(f"o{g}"), 1)
                    for name in DECODE_TILES[h]:
                        wait_full(dve, l, name)
                        if name[:2] == "ds":
                            page_scores(int(name[2:]))
                        elif name == "dn":
                            V_.tensor_tensor(SN[0:NB, :], ps("dn")[0:NB, 0, 0:64], const("newmask", slice(0, NB)), ALU.add)\
                                .then_inc(emptied("dn"), 1)
                            wait_emptied(dve, l, "ds7")
                            wait_emptied(dve, l, "dn")
                            V_.tensor_tensor(M1[0:NB, :], M1[0:NB, :], SN[0:NB, :], ALU.max).then_inc(S["m_all"][0], 1)
                        elif name == "dm":
                            link(V_.tensor_reduce(SMALL[0:64, 8, 0:1], ps("dm")[0:64, 0, 0:P], AX, ALU.max))
                            V_.tensor_scalar(SMALL[0:64, 7, :], const("ident", slice(0, 64), (0, 64)), SMALL[0:64, 8, 0:1],
                                             None, ALU.mult).then_inc(emptied("dm"), 1)
                        elif name == "db":
                            V_.tensor_copy(MB, ps("db")[:, 0, 0:64]).then_inc(emptied("db"), 1)
                            wait_emptied(dve, l, "db")
                            V_.tensor_tensor(PN[0:NB, :], SN[0:NB, :], MB[0:NB, :], ALU.subtract).then_inc(S["sn_sub"][0], 1)
                            for a in range(2):
                                pd = PD[:, 512 * a:512 * a + 512].rearrange("p (b j h) -> p b j h", b=4, j=N_PAGES)
                                mb = MB[:, 32 * a:32 * a + 32].rearrange("p (b o h) -> p b o h", b=4, o=1)
                                i = V_.tensor_tensor(pd, pd, mb.broadcast_to([P, 4, N_PAGES, MH]), ALU.subtract)
                            i.then_inc(S["pd_sub"][0], 1)
                            wait(dve, "pd_ready", l, 1)
                            link(V_.tensor_reduce(RSUM.rearrange("p (b h) -> p b h", b=NB),
                                                  PD[:, :].rearrange("p (b j h) -> p b h j", b=NB, j=N_PAGES), AX, ALU.add))
                            wait(dve, "pd_ready", l, 2)
                            V_.tensor_tensor(RSUM[0:NB, :], RSUM[0:NB, :], PN[0:NB, :], ALU.add).then_inc(S["rsum_ready"][0], 1)
                        elif name == "dd":
                            V_.reciprocal(RD, ps("dd")[:, 0, 0:64]).then_inc(emptied("dd"), 1)
                        elif name[:2] == "dp":
                            b = int(name[2:])
                            dve.sem_inc(pages_used[b % 2], 1)
                            wait_emptied(dve, l, "dd")
                            c = slice(MH * b, MH * b + MH)
                            V_.tensor_tensor(OL[:, c], ps(name)[:, 0, 0:MH], RD[:, c], ALU.mult).then_inc(emptied(name), 1)
                        else:
                            wait(dve, "mix_hi", l, 9)
                            V_.tensor_tensor(XNL[:, 2:6, SEQ:T], ps("dy")[:, 0, 0:4 * NB].rearrange("p (c b) -> p c b", c=4),
                                             XNH[:, 2:6, SEQ:T].bitcast(F32), ALU.subtract).then_inc(emptied("dy"), 1)
                for i, (src, dst) in enumerate(((8, 0), (9, 1), (12, 6), (13, 7))):
                    wait(dve, "mix_hi", l, 10 + i)
                    V_.scalar_tensor_tensor(XNL[:, dst, :], Z[:, src, :], 0.5, XNH[:, dst, :].bitcast(F32),
                                            ALU.mult, ALU.subtract).then_inc(S["mix_lo"][0], 1)
                t0 = TILE_AT["wo0"]
                with dve.Fori(0, KD // 4) as it:
                    for j in range(4):
                        lo(l, U_OUT + j + 2, it, 4)
                        i = t0 + j
                        dve.wait_ge(full_s[i % 4], l * NT4 + it + (i // 4 + 1))
                        xm = X[:, bass.ds(it * 4 + j, 1), :].rearrange("p a (b n) -> p (a b) n", b=2)
                        V_.tensor_tensor(xm, xm, PS[i % 4][:, :, 0:HB], ALU.add).then_inc(emptied_s[i % 4], 1)
                norm(l, "n2", 6, KD, "n2")
                wait(dve, "ffn_free", l, 1)
                settle(dve)
                for hf, (j0, n) in enumerate(HALVES):
                    t0 = TILE_AT[f"up{hf}_0"]
                    with dve.Fori(0, n // 2) as it:
                        for jj in range(2):
                            vi = t0 + 2 * jj + 1
                            c = it * 2 + (j0 + jj)
                            col = it * 2 + (PAR_AT["fcw"][0] + j0 + jj)
                            w = lambda k: PAR[:, bass.ds(col + k * NJ, 1)]
                            fb = lambda k: PAR[:, bass.ds(it * 32 + (PAR_AT["fbuf"][0] + 16 * (j0 + jj) + 8 * k), NB)]
                            y = YC[:, jj, :]
                            wait(dve, "gb_ready", l, c + 1)
                            V_.tensor_copy(FOUT[:, bass.ds(c, 1), :].rearrange("p a n -> p (a n)"), GB[:, jj, SEQ:T + 2])\
                                .then_inc(S["fout_ready"][0], 1)
                            gi = t0 + 2 * jj
                            dve.wait_ge(emptied_s[gi % 4], l * NT4 + it + (gi // 4 + 1 + CREDIT))
                            for k in (1, 0):
                                V_.scalar_tensor_tensor(y[:, SEQ:T], fb(k), w(k), y[:, SEQ:T], ALU.mult, ALU.add)\
                                    .then_inc(S["conv_step"][0], 1)
                                i = V_.scalar_tensor_tensor(y[:, 0:SEQ], GB[:, jj, k:k + SEQ], w(k), y[:, 0:SEQ], ALU.mult, ALU.add)
                                if k:
                                    i.then_inc(S["conv_step"][0], 1)
                                    dve.wait_ge(S["conv_step"][0], l * (3 * NJ) + c * 3 + 2)
                                else:
                                    i.then_inc(S["yc_ready"][0], 1)
                            lo(l, U_UP[hf] + 2 * jj + 2, it, 4)
                            wait(dve, "th_ready", l, c + 1)
                            V_.scalar_tensor_tensor(TH[:, jj, :], TH[:, jj, :], 1.0, y, ALU.add, ALU.mult)\
                                .then_inc(S["hf_ready"][0], 1)
                            wait(dve, "hf_ready", l, c + 1)
                            dve.wait_ge(full_s[vi % 4], l * NT4 + it + (vi // 4 + 1))
                            V_.scalar_tensor_tensor(two(HF[:, jj, :]), two(TH[:, jj, :]), 0.5, PS[vi % 4][:, :, 0:HB],
                                                    ALU.mult, ALU.mult).then_inc(emptied_s[vi % 4], 1)
                            lo(l, U_UP[hf] + 2 * jj + 3, it, 4)
                            wait(dve, "hh_ready", l, c + 1)
                            hsl = bass.ds(it * 2 + jj, 1)
                            V_.tensor_tensor(HL[:, hsl, :], HF[:, jj:jj + 1, :], HH[:, hsl, :].bitcast(F32), ALU.subtract)\
                                .then_inc(S["hl_ready"][0], 1)
                    t0 = TILE_AT[f"dn{hf}_0"]

                    def down(it, split_to):
                        for j in range(4):
                            for x in (2 * j, 2 * j + 1):
                                if x < split_to:
                                    lo(l, U_DN[hf] + x + 2, it, 8)
                            i = t0 + j
                            dve.wait_ge(full_s[i % 4], l * NT4 + it + (i // 4 + 1))
                            m = it * 4 + j
                            xm = X[:, bass.ds(m, 1), :] if not isinstance(m, int) else X[:, m:m + 1, :]
                            xm = xm.rearrange("p a (b n) -> p (a b) n", b=2)
                            V_.tensor_tensor(xm, xm, PS[i % 4][:, :, 0:HB], ALU.add).then_inc(emptied_s[i % 4], 1)

                    if hf == 0:
                        with dve.Fori(0, 2) as it:
                            down(it, 8)
                    else:
                        down(0, 8)
                        down(1, 6)
                assert links[0] == D_LINKS, f"DVE_LINKS is {links[0]}"
            lay[0], links[0] = DEPTH, 0
            norm(DEPTH, "n1", 1, 0, "fin", split=False)

        @block.tensor
        def _(pe):
            mm = nc.tensor.matmul

            def product(l, name, us, xh, xl, rows=P, it=None, per=0):
                i = TILE_AT[name]
                a = l * NT4 + i // 4 + CREDIT
                pe.wait_ge(emptied_s[i % 4], a if it is None else a + it)
                total = sum(n for _, n in us)
                kk = 0
                for u, n in us:
                    b = l * (N_UNITS // NHL) + u // NHL + 1 + CREDIT
                    pe.wait_ge(lo_split[u % NHL], b if it is None else b + it * (per // NHL))
                    tables(pe)
                    for k in range(n):
                        wh = WH[:, u % NHL, k * rows:(k + 1) * rows]
                        wl = WL[:, u % NHL, k * rows:(k + 1) * rows]
                        for s, (w, x) in enumerate(((wh, xh), (wh, xl), (wl, xh))):
                            for hb in range(2):
                                last = mm(PS[i % 4][0:rows, hb, 0:HB], w, x(kk)[:, hb * HB:(hb + 1) * HB],
                                          start=(kk == 0 and s == 0), stop=(kk == total - 1 and s == 2))
                        kk += 1
                    last.then_inc(full_s[i % 4] if kk == total else S["mid_used"][0], 1)

            xh = lambda k: XNH[:, k, :]
            xl = lambda k: XNL[:, k, :]

            def tile(l, name):
                wait_tile(pe, l, name)
                tables(pe)

            def halves(name, lhsT, rhs, rows=slice(0, P), start=True, stop=True):
                for hb in range(2):
                    last = mm(ps(name)[rows, hb, 0:HB], lhsT, rhs[:, hb * HB:(hb + 1) * HB], start=start, stop=stop)
                return last

            def sums(l, name, q0, lhs):
                n = SQ_USES[q0][2]
                tile(l, name)
                for k in range(n):
                    wait(pe, "sq_ready", l, q0 + k + 1)
                    tables(pe)
                    last = halves(name, lhs, SQ[:, (q0 + k) % 2, :], start=(k == 0), stop=(k == n - 1))
                    last.then_inc(full(name) if k == n - 1 else S["sq_used"][0], 1)

            def swap(l, name, perm, src, rows=P):
                tile(l, name)
                halves(name, const(perm, slice(0, rows), (0, rows)), src, slice(0, rows)).then_inc(full(name), 1)

            with pe.Fori(0, DEPTH) as l:
                sums(l, "n1", 0, const("ones"))
                wait(pe, "xl_ready", l, KD)
                for u in range(N_IN_U):
                    product(l, f"in{u}", [(u, KD)], xh, xl, 32 if u == Z_KR else P)
                    if u == 4:
                        sums(l, "nckv", 8, const("ones"))
                        sums(l, "ncq", 9, const("ones"))
                tables(pe)
                wait_emptied(pe, l, "in4")
                swap(l, "pkr", "perm32", Z[0:32, Z_KR, :], 32)
                for i, z in enumerate((3, 5, 6, 7)):
                    wait_emptied(pe, l, f"in{z}")
                    swap(l, f"pz{i}", "perm64", Z[:, z, :])
                pe.wait_ge(small_in, l * 80 + 80)
                wait(pe, "cq_normed", l, 3)
                tile(l, "q8")
                for c in range(6):
                    for k in range(2):
                        last = mm(ps("q8")[:, 0, NB * c:NB * c + NB], UQ[:, k, P * c:P * c + P], Z[:, 1 + k, SEQ:T],
                                  start=(k == 0), stop=(k == 1))
                last.then_inc(full("q8"), 1)
                tables(pe)
                wait_emptied(pe, l, "q8")
                tile(l, "pq8")
                mm(ps("pq8")[:, 0, 0:2 * NB], const("perm32"), Q8[:, :, :].rearrange("p a b -> p (a b)"), start=True, stop=True)\
                    .then_inc(full("pq8"), 1)
                tile(l, "ql")
                for h in range(MH):
                    last = mm(ps("ql")[:, 0, NB * h:NB * h + NB], UKT[:, h, :], QS[0:64, h, :], start=True, stop=True)
                last.then_inc(full("ql"), 1)

                def page_scores(b):
                    s, name = b % 2, f"ds{b}"
                    if b == 0:
                        wait(pe, "qrb_ready", l, 4)
                        wait_emptied(pe, l, "ql")
                        settle(pe)
                    wait_tile(pe, l, name)
                    pe.wait_ge(pages_in[s], l * per_layer + (b // 2 + 1) * 16 * 2 * N_PAGES)
                    tables(pe)
                    for j in range(N_PAGES):
                        o = j * MH
                        if j % 4 == 0:
                            mm(ps(name)[:, 0, o:o + 4 * MH], RT[:, s, P * (j // 4):P * (j // 4) + P],
                               QRB[:, b, :, :].rearrange("p g h -> p (g h)"), start=True, stop=False)
                        last = mm(ps(name)[:, 0, o:o + MH], KT[:, s, P * j:P * j + P], QL[:, b, :],
                                  start=False, stop=j % 4 == 3)
                    last.then_inc(full(name), 1)

                per_layer = 16 * (3 * N_PAGES) * (NB // 2)
                page_scores(0)
                page_scores(1)
                for c in range(RG):
                    wait(pe, "conv_done", l, c + 1)
                    for g, n in enumerate("ri"):
                        tile(l, f"g{c}{n}")
                        halves(f"g{c}{n}", WG[:, 2 * g + c, :], Z[:, 10 + c, :]).then_inc(full(f"g{c}{n}"), 1)
                wait(pe, "roped", l, 4)
                wait_emptied(pe, l, "in9")
                idt = const("ident")
                flat = lambda t: t.rearrange("p b h -> p (b h)")
                for n in range(4):
                    t = f"rt{n // 2}"
                    if n % 2 == 0:
                        tile(l, t)
                    for i, z in enumerate((8, 9, 6, 7)):
                        last = nc.tensor.transpose(ps(t)[:, n % 2, P * i:P * i + P], Z[:, z, P * n:P * n + P], idt)
                    if n % 2:
                        last.then_inc(full(t), 1)
                half = lambda h: slice(64 * (h % 2), 64 * (h % 2) + 64)
                for n in range(4):
                    t = f"rs{n // 2}"
                    if n % 2 == 0:
                        tile(l, t)
                    for h in range(RH):
                        o = 256 * (n % 2) + P * (h // 2)
                        last = mm(ps(t)[:, h % 2, o:o + P], Z[half(h), 6 + h // 2, P * n:P * n + P],
                                  Z[half(h), (3, 5)[h // 2], P * n:P * n + P], start=True, stop=True)
                    if n % 2:
                        last.then_inc(full(t), 1)
                wait_emptied(pe, l, "rt1")
                wait(pe, "kw_ready", l, 4)
                tile(l, "kv")
                for n in range(4):
                    for h in range(RH):
                        o = P * n + HD * (h // 2)
                        last = mm(ps("kv")[half(h), 0, o:o + HD], KW[:, n, HD * h:HD * h + HD], VT[:, n, HD * h:HD * h + HD],
                                  start=True, stop=True)
                last.then_inc(full("kv"), 1)
                page_scores(2)
                page_scores(3)
                wait_emptied(pe, l, "rs1")
                wait_emptied(pe, l, "kv")
                wait(pe, "qd_ready", l, 2)
                tile(l, "ro")
                for n in range(4):
                    for h in range(RH):
                        o = 256 * (h % 2) + P * (h // 2)
                        out = ps("ro")[half(h), h // 2, P * n:P * n + P]
                        last = mm(out, VT[:, n, HD * h:HD * h + HD], SM[:, n, o:o + P], start=True, stop=(n == 0))
                        if n:
                            c = h // 2
                            last = mm(out, SS[half(h), n - 1, HD * c:HD * c + HD], QD[half(h), c, P * n:P * n + P],
                                      start=False, stop=True)
                last.then_inc(full("ro"), 1)
                wait(pe, "cq_normed", l, 1)
                tile(l, "dk")
                for i, z in enumerate((6, 7, 8, 9)):
                    nc.tensor.transpose(ps("dk")[0:NB, 0, P * i:P * i + P], Z[:, z, SEQ:T], idt)
                nc.tensor.transpose(ps("dk")[0:NB, 1, 0:P], Z[:, Z_CKV, SEQ:T], idt).then_inc(full("dk"), 1)
                wait(pe, "vm_ready", l, 4)
                wait_emptied(pe, l, "dk")
                tile(l, "du")
                for h in range(RH):
                    last = mm(ps("du")[half(h), h // 2, :], K8V8[:, HD * h:HD * h + HD], VM[:, h, :], start=True, stop=True)
                last.then_inc(full("du"), 1)
                tables(pe)
                wait_emptied(pe, l, "du")
                tile(l, "do")
                for h in range(RH):
                    for b in range(NB):
                        c = h // 2
                        last = mm(ps("do")[half(h), h % 2, NB * c + b:NB * c + b + 1], SD[half(h), c, HD * b:HD * b + HD],
                                  Z[half(h), (3, 5)[c], SEQ + b:SEQ + b + 1], start=True, stop=True)
                last.then_inc(full("do"), 1)
                wait_emptied(pe, l, "ro")
                wait_emptied(pe, l, "do")
                for c in range(2):
                    tile(l, f"gm{c}")
                    halves(f"gm{c}", const("bd64"), Z[:, 8 + c, :]).then_inc(full(f"gm{c}"), 1)
                page_scores(4)
                page_scores(5)
                sums(l, "gv0", 11, const("bd64"))
                sums(l, "gv1", 12, const("bd64"))
                for c in range(2):
                    tile(l, f"qr{c}")
                    for k in range(2):
                        last = mm(ps(f"qr{c}")[:, 0, :], UQ[:, k, 512 + P * c:512 + P * c + P], Z[:, 1 + k, 0:SEQ],
                                  start=(k == 0), stop=(k == 1))
                    last.then_inc(full(f"qr{c}"), 1)
                    wait_emptied(pe, l, f"qr{c}")
                    tile(l, f"pqr{c}")
                    mm(ps(f"pqr{c}")[:, 0, :], const("perm32"), QR[:, c, :], start=True, stop=True).then_inc(full(f"pqr{c}"), 1)
                for n in range(4):
                    t = ("v01", "v23")[n // 2]
                    if n % 2 == 0:
                        tile(l, t)
                    last = mm(ps(t)[:, n % 2, :], Z[:, Z_CKV, P * n:P * n + P], UV[:, :], start=True, stop=True)
                    if n % 2:
                        last.then_inc(full(t), 1)
                wait(pe, "kr_copied", l, 4)
                off = (0, 512, 896, 1152)
                for h in range(MH + 1):
                    if h < MH:
                        p, s = h // 2, (h // 2) % 2
                        if h % 2 == 0:
                            tile(l, f"q{p}")
                            for k in range(2):
                                last = mm(ps(f"q{p}")[:, 0, :], UQ[:, k, P * p:P * p + P], Z[:, 1 + k, 0:SEQ],
                                          start=(k == 0), stop=(k == 1))
                            last.then_inc(full(f"q{p}"), 1)
                            tile(l, f"k{p}")
                            mm(ps(f"k{p}")[:, 0, :], UK[:, P * p:P * p + P], Z[:, Z_CKV, 0:SEQ], start=True, stop=True)\
                                .then_inc(full(f"k{p}"), 1)
                            tables(pe)
                            wait_emptied(pe, l, f"q{p}")
                            wait_emptied(pe, l, f"k{p}")
                            wait(pe, "qk_ready", l, 2 * p + 2)
                        for q in range(4):
                            n = f"s{'AB'[q // 2]}{h}"
                            if q % 2 == 0:
                                tile(l, n)
                            last = mm(ps(n)[:, q % 2, 0:P * (q + 1)], QCs[s][:, h % 2, P * q:P * q + P],
                                      KCs[s][:, h % 2, 0:P * (q + 1)], start=True, stop=True)
                            if q % 2:
                                last.then_inc(full(n), 1)
                    if h:
                        g = h - 1
                        wait(pe, "p_ready", l, g + 1)
                        for kt in range(4):
                            n = f"t{'AB'[kt // 2]}{g}"
                            if kt % 2 == 0:
                                tile(l, n)
                            for q in range(kt, 4):
                                o = P * (q * (q + 1) // 2) + P * kt
                                last = nc.tensor.transpose(ps(n)[:, kt % 2, P * (q - kt):P * (q - kt) + P], PR[:, o:o + P], idt)
                            if kt % 2:
                                last.then_inc(full(n), 1)
                        wait_emptied(pe, l, f"tA{g}")
                        wait_emptied(pe, l, f"tB{g}")
                        if g == 0:
                            wait_emptied(pe, l, "v23")
                        tile(l, f"o{g}")
                        for kt in range(4):
                            w = SEQ - P * kt
                            last = mm(ps(f"o{g}")[half(g), 0, P * kt:SEQ], V[:, kt, HD * g:HD * g + HD],
                                      PTR[:, off[kt]:off[kt] + w], start=(kt == 0), stop=(kt == 3))
                        last.then_inc(full(f"o{g}"), 1)
                    for name in DECODE_TILES[h]:
                        if name[:2] == "ds":
                            page_scores(int(name[2:]))
                        elif name == "dn":
                            tile(l, "dn")
                            mm(ps("dn")[0:NB, 0, 0:64], Z[:, Z_CKV, SEQ:T], flat(QL[:, :, :]), start=True, stop=False)
                            mm(ps("dn")[0:NB, 0, 0:64], Z[0:32, Z_KR, SEQ:T], QRB[0:32, :, 0, :], start=False, stop=True)\
                                .then_inc(full("dn"), 1)
                        elif name == "dm":
                            wait(pe, "m_all", l, 1)
                            wait_tile(pe, l, "dm")
                            settle(pe)
                            nc.tensor.transpose(ps("dm")[0:64, 0, 0:P], SMALL[:, 2, :], idt).then_inc(full("dm"), 1)
                        elif name == "db":
                            wait_emptied(pe, l, "dm")
                            tile(l, "db")
                            mm(ps("db")[:, 0, 0:64], const("ones", slice(0, 64)), SMALL[0:64, 7, :], start=True, stop=True)\
                                .then_inc(full("db"), 1)
                        elif name == "dd":
                            wait(pe, "rsum_ready", l, 1)
                            tile(l, "dd")
                            mm(ps("dd")[:, 0, 0:64], const("ones"), SMALL[:, 4, :], start=True, stop=True).then_inc(full("dd"), 1)
                        elif name[:2] == "dp":
                            b = int(name[2:])
                            s = b % 2
                            wait_tile(pe, l, name)
                            pe.wait_ge(pages_in[s], l * per_layer + (NB // 2) * 16 * 2 * N_PAGES + (b // 2 + 1) * 16 * N_PAGES)
                            tables(pe)
                            mm(ps(name)[:, 0, 0:MH], C8[:, :], SMALL[0:NB, 1, MH * b:MH * b + MH], start=True, stop=False)
                            for j in range(N_PAGES):
                                o = (b * N_PAGES + j) * MH
                                last = mm(ps(name)[:, 0, 0:MH], KT[:, s, P * j:P * j + P], PD[:, o:o + MH],
                                          start=False, stop=j == N_PAGES - 1)
                            last.then_inc(full(name), 1)
                        else:
                            wait_emptied(pe, l, "dp7")
                            tile(l, "dy")
                            for i in range(MH):
                                ol = SMALL[:, 6, :].rearrange("p (b h) -> p h b", b=NB)[:, i, :]
                                last = mm(ps("dy")[half(i), 0, NB * (i // 2):NB * (i // 2) + NB], UV[:, HD * i:HD * i + HD], ol,
                                          start=True, stop=True)
                            last.then_inc(full("dy"), 1)
                with pe.Fori(0, KD // 4) as it:
                    wait(pe, "mix_hi", l, 13)
                    wait(pe, "mix_lo", l, 4)
                    wait_emptied(pe, l, "dy")
                    for j in range(4):
                        product(l, f"wo{j}", [(U_OUT + j, KD)], xh, xl, it=it, per=4)
                sums(l, "n2", 13, const("ones"))
                for hf, (j0, n) in enumerate(HALVES):
                    with pe.Fori(0, n // 2) as it:
                        wait(pe, "xl_ready", l, 2 * KD)
                        for j in range(4):
                            product(l, f"up{hf}_{j}", [(U_UP[hf] + j, KD)], xh, xl, it=it, per=4)
                    with pe.Fori(0, KD // 4) as it:
                        wait(pe, "hl_ready", l, j0 + n + 1)
                        for m in range(4):
                            u = U_DN[hf] + 2 * m
                            product(l, f"dn{hf}_{m}", [(u, n // 2), (u + 1, n // 2)], lambda k: HH[:, k, :],
                                    lambda k: HL[:, k, :], it=it, per=8)
            sums(DEPTH, "n1", 0, const("ones"))


DVE_LINKS = 93
CREDIT = 1
OUTS = [("y", (KD, P, T)), ("lat", (DEPTH, P, T)), ("rope", (DEPTH, 32, T)), ("ret", (DEPTH, P, 2 * HD)),
        ("gx", (DEPTH * RG, P, 11)), ("hr", (DEPTH * RG, P, NB + 1)), ("ff", (DEPTH, P, NJ, 10)),
        ("sret", (DEPTH, P, 2, NB * HD)), ("rgc0", (DEPTH, NB, RGC - 2, 256)), ("ffc0", (DEPTH, NB, 1, D_FF))]


def kernel(**inputs):
    import concourse.bacc as _bacc
    from concourse.bass_utils import run_bass_kernel_spmd as _run

    a = {k: np.asarray(v) for k, v in inputs.items()}
    D = DEPTH
    f32 = np.float32

    def unit(w, cols):
        d, rows, n = w.shape
        u = w.reshape(d, rows // P, P, n // cols, cols).transpose(0, 3, 2, 1, 4).reshape(d, n // cols, P, -1)
        return np.concatenate([u, np.zeros(u.shape[:3] + (UW - u.shape[3],), f32)], 3)

    w_in = a["w_in"]
    z_cols = [1280, 1024, 1152, 0, 1408, 128, 256, 384, 512, 640, 1440, 1568, 1696, 1824, 768, 896]
    parts = [unit(w_in[:, :, c:c + (32 if i == Z_KR else P)], 32 if i == Z_KR else P) for i, c in enumerate(z_cols)]
    parts.append(unit(a["w_out"], P))
    up, dn = a["ffn_w_up"], a["ffn_w_down"]
    for j0, n in HALVES:
        g = unit(up[:, :, j0 * P:(j0 + n) * P], P)
        v = unit(up[:, :, D_FF + j0 * P:D_FF + (j0 + n) * P], P)
        parts.append(np.stack([g, v], 2).reshape(D, 2 * n, P, UW))
        m = n // 2
        two = [unit(dn[:, (j0 + i * m) * P:(j0 + (i + 1) * m) * P, :], P) for i in range(2)]
        parts.append(np.stack(two, 2).reshape(D, 2 * KD, P, UW))
    units = np.concatenate(parts, 1).reshape(D * N_UNITS, P, UW)

    cols = lambda x, n: x.reshape(D, n, P).transpose(0, 2, 1)
    par = {
        "n1": cols(a["norm1_w"], KD), "n2": cols(a["norm2_w"], KD), "qn": cols(a["mla_q_norm_w"], 2),
        "kn": cols(a["mla_kv_norm_w"], 1), "gn": cols(a["ret_gn_w"], 2),
        "rcw": a["rg_conv_w"].reshape(D, RGC, RG, P).transpose(0, 3, 2, 1), "rcb": cols(a["rg_conv_b"], RG),
        "ba": cols(a["rg_b_a"], RG), "bx": cols(a["rg_b_x"], RG), "lam": cols(a["rg_lambda"], RG),
        "fcw": a["ffn_conv_w"].reshape(D, 3, NJ, P).transpose(0, 3, 1, 2), "fcb": cols(a["ffn_conv_b"], NJ),
        "cbuf": a["state_rg_conv"].reshape(D, NB, RGC - 1, RG, P).transpose(0, 4, 3, 2, 1),
        "h0": a["state_rglru"].reshape(D, NB, RG, P).transpose(0, 3, 2, 1),
        "fbuf": a["state_ffn_conv"].reshape(D, NB, 2, NJ, P).transpose(0, 4, 3, 2, 1),
        "fin": np.broadcast_to(a["final_norm_w"].reshape(1, KD, P).transpose(0, 2, 1), (D, P, KD)),
    }
    par = np.concatenate([par[n].reshape(D, P, w) for n, w in PAR_W], 2)
    x = np.concatenate([a["x_prompt"].reshape(SEQ, D_MODEL), a["x_sample"].reshape(NB, D_MODEL)], 0)
    uq = a["mla_w_uq"].reshape(D, 2, P, MH, 96)
    uq = np.concatenate([uq[..., :64].reshape(D, 2, P, 512), uq[..., 64:].reshape(D, 2, P, 256)], 3)
    wg = np.zeros((D, P, 4, P), f32)
    for g, n in enumerate(("rg_w_a", "rg_w_x")):
        for blk in range(4):
            r = slice(64 * (blk % 2), 64 * (blk % 2) + 64)
            wg[:, r, 2 * g + blk // 2, r] = a[n][:, blk]
    lat = a["cache_mla_latent"]
    ins = {
        "units": units, "const": constants(), "par": par, "x": x.T.reshape(KD, P, T),
        "uq": uq.transpose(0, 2, 1, 3), "uk": a["mla_w_uk"].reshape(D, P, 512),
        "ukt": a["mla_w_uk"].transpose(0, 3, 2, 1), "uv": a["mla_w_uv"].reshape(D, P, 512), "wg": wg,
        "s0": a["state_ret"].reshape(D, NB, 2, 2, HD, HD).transpose(0, 3, 4, 2, 1, 5).reshape(D, P, 2, NB * HD),
        "kat": lat.transpose(0, 1, 3, 2).reshape(D * N_PHYS, P, P),
        "kar": a["cache_mla_krope"].transpose(0, 1, 3, 2).reshape(D * N_PHYS, 32, P),
        "ka": lat.reshape(D * N_PHYS, P, P), "pt": a["page_table"].reshape(1, NB * N_PAGES),
        "cp": a["state_rg_conv"][:, :, 1:], "fp": a["state_ffn_conv"][:, :, 1:],
    }
    nc = _bacc.Bacc("TRN2", target_bir_lowering=False, num_devices=1)
    arrays, args = {}, []
    for name, v in ins.items():
        v = np.ascontiguousarray(v)
        arrays[f"in_{name}"] = v
        args.append(nc.dram_tensor(f"in_{name}", v.shape, mybir.dt.from_np(v.dtype), kind="ExternalInput").ap())
    for name, shape in OUTS:
        args.append(nc.dram_tensor(f"out_{name}", shape, F32, kind="ExternalOutput").ap())
    build(nc, *args)
    r = _run(nc, [arrays], core_ids=[0]).results[0]
    o = {name: np.asarray(r[f"out_{name}"]) for name, _ in OUTS}

    y = o["y"].reshape(D_MODEL, T).T
    latT, ropeT = o["lat"].transpose(0, 2, 1), o["rope"].transpose(0, 2, 1)
    gx = o["gx"].reshape(D, RG * P, 11).transpose(0, 2, 1)
    hr = o["hr"].reshape(D, RG * P, NB + 1).transpose(0, 2, 1)
    ff = o["ff"].transpose(0, 3, 2, 1).reshape(D, 10, D_FF)
    ret = o["ret"].reshape(D, 2, HD, 2, HD).transpose(0, 3, 1, 2, 4).reshape(D, 1, RH, HD, HD)
    sret = o["sret"].reshape(D, 2, HD, 2, NB, HD).transpose(0, 4, 3, 1, 2, 5).reshape(D, NB, RH, HD, HD)
    c = np.ascontiguousarray
    return (c(y[None, :SEQ]), c(y[SEQ:, None]), c(latT[:, None, :SEQ]), c(ropeT[:, None, :SEQ]), c(ret),
            c(gx[:, None, 0:3]), c(hr[:, None, 0]), c(ff[:, None, 0:2]), c(latT[:, SEQ:, None]), c(ropeT[:, SEQ:, None]),
            c(sret), np.concatenate([o["rgc0"], gx[:, 3:, None]], 2), c(hr[:, 1:]),
            np.concatenate([o["ffc0"], ff[:, 2:, None]], 2))
```

```python
from contextlib import ExitStack

import concourse.bass as bass
import numpy as np
from concourse import mybir

F32 = mybir.dt.float32
F32R = mybir.dt.float32r
I32 = mybir.dt.int32
ACT = mybir.ActivationFunctionType
ALU = mybir.AluOpType
AX = mybir.AxisListType.X

P = 128
D_MODEL, SEQ, DEPTH, NB = 1024, 512, 2, 8
T = SEQ + NB
HB = T // 2
KD = D_MODEL // P
PAGE, N_PAGES, N_PHYS, PAST = 128, 16, 160, 2048
RH, HD = 4, 64
MH, ROPE_D, KVR, QR_ = 8, 32, 128, 256
RG, RGC = 2, 4
D_FF = 2816
NJ = D_FF // P
EPS = 1e-6
SCALE = (64 + 32) ** -0.5
NEG = -1e30
G_C1, G_C2 = 0.044715, float(np.sqrt(2.0 / np.pi))
HALVES = ((0, 12), (12, 10))

Z_CKV, Z_CQ, Z_RQ, Z_KR, Z_RK, Z_RV, Z_GX, Z_GG, Z_GATE = 0, (1, 2), (3, 5), 4, (6, 7), (8, 9), (10, 11), (12, 13), (14, 15)
N_IN_U = 16
ORDER = (10, 11, 12, 13, 0, 1, 2, 4, 3, 5, 6, 7, 8, 9, 14, 15)
U_KR = ORDER.index(Z_KR)
U_OUT = N_IN_U
U_UP = [0, 0]
U_DN = [0, 0]
U_UP[0] = U_OUT + KD
U_DN[0] = U_UP[0] + 2 * HALVES[0][1]
U_UP[1] = U_DN[0] + 2 * KD
U_DN[1] = U_UP[1] + 2 * HALVES[1][1]
N_UNITS = U_DN[1] + 2 * KD
NRAW, NHL = 4, 2
UW = KD * P

MIX_ROWS = {MH - 1: ((8, 0), (9, 1)), MH: ((12, 6), (13, 7))}
DECODE_TILES = [["ds6"], ["ds7", "dn", "dm"], ["db"], ["dd", "dp0", "dp1"], ["dp2"], ["dp3"], ["dp4", "dp5"],
                ["dp6"], ["dp7", "dy"]]
TILES = [f"in{z}" for z in ORDER]
for _at, _names in ((9, ["nckv", "ncq"]), (8, ["g1r", "g1i"]), (7, ["g0r", "g0i"]), (1, ["n1"])):
    TILES[_at:_at] = _names
TILES += ["pkr"] + [f"pz{i}" for i in range(4)]
TILES += ["q8", "pq8", "ql", "ds0", "ds1"]
TILES += ["rt0", "rt1", "rs0", "rs1", "kv", "ds2", "ro", "dk", "du", "do", "ds3"]
TILES += ["gm0", "gm1", "gv0", "gv1", "ds4"]
TILES += ["qr0", "pqr0", "qr1", "pqr1", "ds5", "v01", "v23"]
for _h in range(MH + 1):
    if _h < MH:
        if _h % 2 == 0:
            TILES += [f"q{_h // 2}", f"k{_h // 2}"]
        TILES += [f"sA{_h}", f"sB{_h}"]
    if _h:
        TILES += [f"tA{_h - 1}", f"tB{_h - 1}"]
    TILES += DECODE_TILES[_h] + [f"o{_h - 1}"] * (_h > 0)
TILES += [f"wo{m}" for m in range(KD)] + ["n2"]
for _i, (_j0, _n) in enumerate(HALVES):
    TILES += [f"up{_i}_{j}" for j in range(2 * _n)] + [f"dn{_i}_{m}" for m in range(KD)]
assert len(TILES) % 4 == 0
TILE_AT = {name: i for i, name in enumerate(TILES)}
NT4 = len(TILES) // 4

SQ_USES = [("nckv", 0, 1), ("ncq", 0, 2), ("ncq", 1, 2), ("gv0", 0, 1), ("gv1", 0, 1)]
SQ_MID = [sum(k < n - 1 for _, k, n in SQ_USES[:i]) for i in range(len(SQ_USES) + 1)]

CONST_W = [("ident", 128), ("ones", 128), ("bd64", 128), ("perm64", 128), ("perm32", 128),
           ("cosr", T), ("sinr", T), ("cosm", T), ("sinm", T), ("decay", 512), ("gq", 256), ("wk", 256),
           ("gam", 4), ("causal", 128), ("newmask", 64), ("bmask", 512), ("zero", 4)]
CONST_AT, _o = {}, 0
for _n_, _w in CONST_W:
    CONST_AT[_n_] = (_o, _w)
    _o += _w
CONST_N = _o
PAR_W = [("n2", 8), ("qn", 2), ("kn", 1), ("gn", 2), ("rcw", 8), ("rcb", 2), ("ba", 2), ("bx", 2),
         ("lam", 2), ("fcw", 3 * NJ), ("fcb", NJ), ("cbuf", 48), ("h0", 16), ("fbuf", NJ * 16)]
PAR_AT, _o = {}, 0
for _n_, _w in PAR_W:
    PAR_AT[_n_] = (_o, _w)
    _o += _w
PAR_N = _o


def constants():
    c = {n: np.zeros((P, w), np.float32) for n, w in CONST_W}
    f32 = np.float32
    pos = np.concatenate([np.arange(SEQ), np.full(NB, PAST)]).astype(f32)
    p = np.arange(P)
    c["ident"][:] = np.eye(P)
    c["ones"][:] = 1.0
    c["bd64"][:] = np.kron(np.eye(2), np.ones((64, 64))) / 64.0
    for name, half, cn, sn in (("perm64", 32, "cosr", "sinr"), ("perm32", 16, "cosm", "sinm")):
        c[name][p ^ half, p] = 1.0
        freqs = (f32(10000.0) ** (-np.arange(half, dtype=f32) / f32(half))).astype(f32)
        ang = (pos[None, :] * freqs[p % half][:, None]).astype(f32)
        c[cn][:] = np.cos(ang)
        c[sn][:] = np.where((p // half % 2 == 0)[:, None], -np.sin(ang), np.sin(ang))
    lg = np.log(1.0 - 2.0 ** (-5.0 - np.arange(RH)))
    i = np.arange(P)
    rel = i[None, :] - i[:, None]
    for h in range(RH):
        o = (2 * (h % 2) + h // 2) * P
        c["decay"][:, o:o + P] = np.where(rel >= 0, np.exp(lg[h] * np.maximum(rel, 0)), 0)
        c["wk"][:, h * HD:(h + 1) * HD] = np.exp(lg[h] * (P - 1.0 - i))[:, None]
        rows = slice(64 * (h % 2), 64 * (h % 2) + 64)
        c["gq"][rows, (h // 2) * P:(h // 2 + 1) * P] = np.exp(lg[h] * (i + 1.0))[None]
        c["gam"][rows, h // 2] = np.exp(lg[h] * P)
        c["gam"][rows, 2 + h // 2] = np.exp(lg[h])
    c["causal"][:] = np.where(i[None, :] <= i[:, None], 0.0, NEG)
    b = np.arange(NB)
    c["newmask"][:NB] = np.where(np.repeat(b, MH)[None] == b[:, None], 0.0, NEG)
    c["bmask"][:NB] = (np.repeat(b, HD)[None] == b[:, None])
    return np.concatenate([c[n] for n, _ in CONST_W], 1)


def build(nc, units, constd, pard, nwd, xd, uqd, ukd, uktd, uvd, wgd, s0d, katd, karp, kav, ptd, cpd, fpd,
          y_o, lat_o, rope_o, pret_o, gx_o, hr_o, ff_o, sret_o, rgc0_o, ffc0_o):
    ctx = ExitStack()
    with ctx:
        sem = lambda name: ctx.enter_context(nc.semaphore(name))
        cursor = [(nc.sbuf_base + 31) // 32 * 32]

        def over(name, shape, dt=F32, at=None):
            size = (4 * int(np.prod(shape[1:])) + 31) // 32 * 32
            o = cursor[0] if at is None else at
            if at is None:
                cursor[0] += size
            assert o + size <= nc.sbuf_usable_end, (name, o + size - nc.sbuf_usable_end)
            return nc.alloc_sbuf_tensor_at(name, shape, dt, offset=o, align_bytes=32)

        X = over("X", [P, KD, T])
        xnh0 = cursor[0]
        XNH = over("XNH", [P, KD, T], F32R)
        xnl0 = cursor[0]
        XNL = over("XNL", [P, KD, T], F32R)
        raw0 = cursor[0]
        RAW = over("RAW", [P, NRAW, UW])
        WH = over("WH", [P, NHL, UW], F32R)
        WL = over("WL", [P, NHL, UW], F32R)
        C = over("C", [P, CONST_N])
        PAR = over("PAR", [P, PAR_N])
        RGP = over("RGP", [P, 32])
        SQ = over("SQ", [P, 2, T])
        XF = over("XF", [P, 2, T])
        RS = over("RS", [P, T])
        QS = over("QS", [96, MH, NB])
        Q8 = over("Q8", [P, 2, NB])
        QL = over("QL", [P, NB, MH])
        QRB = over("QRB", [P, NB, 4, MH])
        NW = over("NW", [P, (DEPTH + 1) * KD])
        PT_SB = over("PT_SB", [1, NB * N_PAGES], I32)
        ACC = XF[:, 1, :]
        STAT = over("STAT", [P, 16])
        base = cursor[0]

        Z = over("Z", [P, 16, T])
        GXB = over("GXB", [P, RG, T + 8])
        qr0 = cursor[0]
        QR = over("QR", [P, 2, SEQ])
        SD = over("SD", [P, 2, NB * HD], at=qr0)
        UQ = over("UQ", [P, 2, 768])
        UK = over("UK", [P, 512])
        UKT = over("UKT", [64, MH, P])
        UV = over("UV", [P, 512])
        WG = over("WG", [P, 4, P])
        KT = over("KT", [P, 2, N_PAGES * P])
        RT = over("RT", [P, 2, 4 * P])
        gbase = cursor[0]
        PR = over("PR", [P, 1280])
        PTR = over("PTR", [P, 1280])
        V = over("V", [P, 4, 512])
        R = [over(f"R{i}", [P, T], at=gbase + 2080 * i) for i in range(8)]
        SM = over("SM", [P, 4, 512], at=gbase)
        VM = over("VM", [NB, RH, NB * HD], at=gbase + 8192)
        K8V8 = over("K8V8", [NB, 512], at=gbase + 16384)
        O8 = over("O8", [MH, NB * P], at=raw0 + 8 * UW)
        PD = over("PD", [P, NB * N_PAGES * MH], at=raw0)
        SMALL = over("SMALL", [P, 10, 64], at=raw0 + 4 * UW)
        C8 = over("C8", [NB, P], at=raw0 + 4 * UW + 4 * 640)
        VT = over("VT", [P, 4, 256], at=xnh0)
        KW = over("KW", [P, 4, 256], at=xnh0 + 6 * T * 4)
        QD = over("QD", [P, 2, 512], at=xnl0)
        SS = over("SS", [P, 4, 2 * HD], at=xnl0 + 6 * T * 4)
        QCs = [over(f"QC{i}", [96, 2, SEQ], at=xnh0 + i * 6 * T * 4) for i in range(2)]
        KCs = [over(f"KC{i}", [96, 2, SEQ], at=xnl0 + i * 6 * T * 4) for i in range(2)]
        cursor[0] = base
        HH = over("HH", [P, 12, T], F32R)
        HL = over("HL", [P, 12, T], F32R)
        GB = over("GB", [P, 2, T + 8])
        YC = over("YC", [P, 2, T])
        TH = over("TH", [P, 2, T])
        HF = over("HF", [P, 2, T])
        FOUT = over("FOUT", [P, NJ, 10])

        PS = [ctx.enter_context(nc.psum_tensor(f"PS{i}", [P, 2, 512], F32)) for i in range(4)]

        tables_in, pars_in, x_in, pt_in = sem("tables_in"), sem("pars_in"), sem("x_in"), sem("pt_in")
        small_in, sd_in = sem("small_in"), sem("sd_in")
        raw_full = [sem(f"raw_full{i}") for i in range(NRAW)]
        hi_split = [sem(f"hi_split{i}") for i in range(NHL)]
        lo_split = [sem(f"lo_split{i}") for i in range(NHL)]
        full_s = [sem(f"full{i}") for i in range(4)]
        emptied_s = [sem(f"emptied{i}") for i in range(4)]
        pages_in = [sem(f"pages_in{i}") for i in range(2)]
        pages_used = [sem(f"pages_used{i}") for i in range(2)]
        names = {"sq_ready": 5, "sq_used": SQ_MID[-1], "std_ready": 6, "xf_ready": 0, "xsq_ready": 16,
                 "xsq_added": 16, "xh_ready": 16, "xl_ready": 16,
                 "mid_used": 16, "roped": 6, "cq_normed": 3, "kr_roped": 1, "zeroed": 1, "acc_zero": 1,
                 "conv_done": 2, "rgp_half": 1, "lam_exp": 1, "lam_abs": 1, "q_ready": 2,
                 "tau_ready": 2, "a_ready": 2, "m_ready": 2, "g_ready": 2, "gl_sq": 2, "gl_arg": 2, "gl_tanh": 2,
                 "rg_done": 2, "kw_ready": 4, "qd_ready": 2, "vm_ready": 4, "gt_ready": 2, "gt_silu": 2, "ret_done": 2,
                 "mix_hi": 9, "mixr_hi": 4, "mix_lo": 4, "qk_ready": 8, "kr_copied": 4, "nmax_ready": 8, "p_ready": 8,
                 "qs_ready": 4, "qrb_ready": 4, "m_all": 1, "sn_sub": 1, "pd_sub": 1, "ot_ready": 1, "ol_ready": 1, "pd_ready": 2, "rsum_ready": 1,
                 "y0_ready": NJ, "fout_ready": NJ, "conv_step": 3 * NJ, "yc_ready": NJ, "yr_ready": NJ, "th_ready": NJ, "hf_ready": NJ,
                 "hh_ready": NJ, "hl_ready": NJ, "saved": 16 * 11, "ffn_free": 1}
        S = {n: (sem(n), k) for n, k in names.items()}
        pt_clamped = sem("pt_clamped")
        settled, layers_saved = sem("settled"), sem("layers_saved")
        dve_chain, y_saved = sem("dve_chain"), [sem(f"y_saved{i}") for i in range(2)]

        def wait(e, name, l, c):
            s, per = S[name]
            e.wait_ge(s, (0 if l is None else l * per) + c + (CREDIT if name == "hl_ready" else 0))

        def const(name, rows=slice(0, P), cols=None):
            o, w = CONST_AT[name]
            a, b = cols or (0, w)
            return C[rows, o + a:o + b]

        def par(name, a=0, b=None, rows=slice(0, P)):
            o, w = PAR_AT[name]
            return PAR[rows, o + a:o + (w if b is None else b)]

        def wait_full(e, l, name):
            i = TILE_AT[name]
            e.wait_ge(full_s[i % 4], l * NT4 + i // 4 + 1)

        def wait_emptied(e, l, name):
            i = TILE_AT[name]
            e.wait_ge(emptied_s[i % 4], l * NT4 + i // 4 + 1 + CREDIT)

        def wait_tile(e, l, name):
            i = TILE_AT[name]
            e.wait_ge(emptied_s[i % 4], l * NT4 + i // 4 + CREDIT)

        ps = lambda name: PS[TILE_AT[name] % 4]
        full = lambda name: full_s[TILE_AT[name] % 4]
        emptied = lambda name: emptied_s[TILE_AT[name] % 4]
        two = lambda ap: ap.rearrange("p (a n) -> p a n", a=2)
        psT = lambda name, r=slice(0, P): ps(name)[r, :, 0:HB]
        plain = lambda e: e.wait_ge(x_in, 16 * (KD + 1))
        settle = lambda e: e.sem_inc(settled, 1)

        def rings_split(e, l, u):
            e.wait_ge(lo_split[u % NHL], l * (N_UNITS // NHL) + u // NHL + 1 + CREDIT)

        def before_layer(e, l):
            e.wait_ge(emptied_s[TILE_AT[f"dn1_{KD - 1}"] % 4], l * NT4 + CREDIT)

        block = ctx.enter_context(nc.Block())

        @block.sync
        def _(sp):
            sp.dma_start(PT_SB[:, :], ptd).then_inc(pt_in, 16)
            for s in lo_split + emptied_s + pages_used + [S["mid_used"][0]]:
                sp.sem_inc(s, CREDIT)
            for k in range(KD):
                sp.dma_start(X[:, k, :], xd[k]).then_inc(x_in, 16)
            sp.dma_start(NW[:, :], nwd).then_inc(x_in, 16)
            sp.wait_ge(pt_clamped, 1)

            def unit_wait(l, u):
                if u >= NRAW:
                    v = u - NRAW
                    sp.wait_ge(lo_split[v % NHL], l * (N_UNITS // NHL) + v // NHL + 1 + CREDIT)
                else:
                    sp.wait_ge(lo_split[u % NHL], l * (N_UNITS // NHL) + CREDIT)

            def one(l, u, width=UW):
                unit_wait(l, u)
                src = units[bass.ds(l * N_UNITS + u, 1), :, 0:width].rearrange("a p n -> p (a n)")
                sp.dma_start(RAW[:, u % NRAW, 0:width], src).then_inc(raw_full[u % NRAW], 16)

            def slot_free(l, phase, bp, s):
                sp.wait_ge(pages_used[s], l * NB + phase * (NB // 2) + bp + CREDIT)
                settle(sp)

            def four_pages(l, phase, bp, s, j0):
                at = bp * (2 * N_PAGES) + (s * N_PAGES + j0)
                _, numbers = nc.values_load_multi_w_load_instructions(
                    PT_SB[0:1, bass.ds(at, 4)], engines=[mybir.EngineType.SP], min_val=0, max_val=N_PHYS - 1,
                    skip_runtime_bounds_check_because="Vector has clamped the page numbers to the pool")
                for j, page in enumerate(numbers, j0):
                    row = l * N_PHYS + page
                    sp.dma_start(KT[:, s, j * P:(j + 1) * P],
                                 (katd, kav)[phase][bass.ds(row, 1), :, :].rearrange("a p n -> p (a n)"))\
                        .then_inc(pages_in[s], 16)
                    if phase == 0:
                        g = 32 * (j % 4)
                        sp.dma_start(RT[g:g + 32, s, (j // 4) * P:(j // 4 + 1) * P],
                                     karp[bass.ds(row, 1), :, :].rearrange("a p n -> p (a n)"))\
                            .then_inc(pages_in[s], 16)

            def pages(l, phase, bp):
                for s in range(2):
                    slot_free(l, phase, bp, s)
                    for j0 in range(0, N_PAGES, 4):
                        four_pages(l, phase, bp, s, j0)

            with sp.Fori(0, DEPTH) as l:
                for u in range(NRAW + 1):
                    one(l, u)
                before_layer(sp, l)
                settle(sp)
                sp.wait_ge(layers_saved, l + CREDIT)
                settle(sp)
                slot_free(l, 0, 0, 0)
                slot_free(l, 0, 0, 1)
                for u in range(NRAW + 1, N_IN_U + 2):
                    one(l, u, 256 if u == U_KR else UW)
                    g = u - (NRAW + 1)
                    if g < 2 * (N_PAGES // 4):
                        four_pages(l, 0, 0, g // 4, 4 * (g % 4))
                with sp.Fori(0, NB // 2 - 1) as bp:
                    pages(l, 0, bp + 1)
                with sp.Fori(0, NB // 2) as bp:
                    pages(l, 1, bp)
                wait_full(sp, l, "dy")
                settle(sp)
                for u in range(N_IN_U + 2, U_UP[0]):
                    one(l, u)
                for u0, n, w in ((U_UP[0], 2 * HALVES[0][1], UW), (U_DN[0], 2 * KD, 6 * P),
                                 (U_UP[1], 2 * HALVES[1][1], UW), (U_DN[1], 2 * KD, 5 * P)):
                    with sp.Fori(0, n // NRAW) as it:
                        for j in range(NRAW):
                            v = u0 + j - NRAW
                            sp.wait_ge(lo_split[v % NHL], l * (N_UNITS // NHL) + it * (NRAW // NHL) + v // NHL + 1 + CREDIT)
                            row = l * N_UNITS + it * NRAW + (u0 + j)
                            sp.dma_start(RAW[:, (u0 + j) % NRAW, 0:w],
                                         units[bass.ds(row, 1), :, 0:w].rearrange("a p n -> p (a n)"))\
                                .then_inc(raw_full[(u0 + j) % NRAW], 16)

        @block.gpsimd
        def _(pool):
            pool.wait_ge(x_in, 16 * (KD + 1))
            pool.dma_start(C[:, :], constd).then_inc(tables_in, 16)
            pool.sem_inc(layers_saved, CREDIT)
            with pool.Fori(0, DEPTH) as l:
                plain(pool)
                before_layer(pool, l)
                pool.dma_start(PAR[:, :], pard[bass.ds(l, 1)].rearrange("a p n -> p (a n)")).then_inc(pars_in, 16)
                for dst, src in ((UQ[:, :, :], uqd), (UK[:, :], ukd), (UKT[:, :, :], uktd), (UV[:, :], uvd),
                                 (WG[:, :, :], wgd)):
                    s = src[bass.ds(l, 1)]
                    s = s.rearrange("a p k n -> p (a k) n") if len(dst.shape) == 3 else s.rearrange("a p n -> p (a n)")
                    pool.dma_start(dst, s).then_inc(small_in, 16)
                pool.dma_start(SD[:, :, :], s0d[bass.ds(l, 1)].rearrange("a p k n -> p (a k) n")).then_inc(sd_in, 16)
                saved = S["saved"][0]
                pool.dma_start(rgc0_o[bass.ds(l, 1)], cpd[bass.ds(l, 1)]).then_inc(saved, 16)
                pool.dma_start(ffc0_o[bass.ds(l, 1)], fpd[bass.ds(l, 1)]).then_inc(saved, 16)
                sl = lambda o: o[bass.ds(l, 1)].rearrange("a p n -> p (a n)")
                wait(pool, "cq_normed", l, 1)
                pool.dma_start(sl(lat_o), Z[:, Z_CKV, :]).then_inc(saved, 16)
                wait(pool, "kr_roped", l, 1)
                pool.dma_start(sl(rope_o), Z[0:32, Z_KR, :]).then_inc(saved, 16)
                wait_emptied(pool, l, "in10")
                pool.dma_start(gx_o[bass.ds(2 * l, 1)].rearrange("a p n -> p (a n)"), GXB[:, 0, SEQ:T + 3]).then_inc(saved, 16)
                wait_emptied(pool, l, "in11")
                pool.dma_start(gx_o[bass.ds(2 * l + 1, 1)].rearrange("a p n -> p (a n)"), GXB[:, 1, SEQ:T + 3]).then_inc(saved, 16)
                wait(pool, "rg_done", l, 1)
                pool.dma_start(hr_o[bass.ds(2 * l, 1)].rearrange("a p n -> p (a n)"), Z[:, 10, SEQ - 1:T]).then_inc(saved, 16)
                wait(pool, "rg_done", l, 2)
                pool.dma_start(hr_o[bass.ds(2 * l + 1, 1)].rearrange("a p n -> p (a n)"), Z[:, 11, SEQ - 1:T]).then_inc(saved, 16)
                wait_emptied(pool, l, "kv")
                pool.dma_start(sl(pret_o), SS[:, 3, :]).then_inc(saved, 16)
                wait_emptied(pool, l, "du")
                settle(pool)
                pool.dma_start(sret_o[bass.ds(l, 1)].rearrange("a p k n -> p (a k) n"), SD[:, :, :]).then_inc(saved, 16)
                wait(pool, "fout_ready", l, NJ)
                pool.dma_start(ff_o[bass.ds(l, 1)].rearrange("a p k n -> p (a k) n"), FOUT[:, :, :]).then_inc(saved, 16)
                wait(pool, "saved", l, 16 * 11)
                pool.sem_inc(layers_saved, 1)
            for k in range(KD):
                wait(pool, "xf_ready", DEPTH, k + 1)
                pool.dma_start(y_o[k], XF[:, k % 2, :]).then_inc(y_saved[k % 2], 16)
            pool.wait_ge(y_saved[0], 16 * KD // 2)
            pool.wait_ge(y_saved[1], 16 * KD // 2)

        @block.scalar
        def _(act):
            def hi(l, u, it=None, tile=None, mid=None):
                a = l * (N_UNITS // NRAW) + u // NRAW + 1
                if it is not None:
                    a = a + it * (1 if u < U_DN[0] or U_UP[1] <= u < U_DN[1] else 2)
                act.wait_ge(raw_full[u % NRAW], a * 16)
                if mid is not None:
                    b = l * S["mid_used"][1] + mid + CREDIT
                    act.wait_ge(S["mid_used"][0], b if it is None else b + it * 4)
                elif tile is not None:
                    b = l * NT4 + TILE_AT[tile] // 4 + 1
                    act.wait_ge(full_s[TILE_AT[tile] % 4], b if it is None else b + it)
                plain(act)
                act.activation(WH[:, u % NHL, :], RAW[:, u % NRAW, :], ACT.Copy).then_inc(hi_split[u % NHL], 1)

            def hi_down(l, hf, x, it=None):
                m = x // 2
                u = U_DN[hf] + x + 2
                if x % 2 == 0:
                    hi(l, u, it, mid=8 * hf + m + 1)
                else:
                    hi(l, u, it, tile=f"dn{hf}_{m}")

            def square_free(l, q):
                if q < 2:
                    wait(act, "xsq_added", l, KD)
                else:
                    t, k, n = SQ_USES[q - 2]
                    if k < n - 1:
                        wait(act, "sq_used", l, SQ_MID[q - 1])
                    else:
                        wait_full(act, l, t)

            def squares(l, q0, aps, before):
                for k, ap in enumerate(aps):
                    before(k)
                    q = q0 + k
                    square_free(l, q)
                    act.activation(SQ[:, q % 2, :], ap, ACT.Square).then_inc(S["sq_ready"][0], 1)

            def root(l, name, rs=RS[:, :]):
                wait_emptied(act, l, name)
                act.activation(rs, rs, ACT.Sqrt).then_inc(S["std_ready"][0], 1)

            def chunk(l, c0, k, weight, ready):
                ready()
                if k >= 2:
                    wait(act, "xsq_added", l, c0 + k - 1)
                elif l is not None:
                    wait(act, "xsq_added", l, c0)
                act.activation(SQ[:, k % 2, :], X[:, k, :], ACT.Square).then_inc(S["xsq_ready"][0], 1)
                ready()
                act.activation(XNH[:, k, :], X[:, k, :], ACT.Copy, scale=weight).then_inc(S["xh_ready"][0], 1)

            def next_weight(l, k):
                return NW[:, k:k + 1] if l is None else NW[:, bass.ds(l * KD + (KD + k), 1)]

            def evac(l, name, dst, src, **kw):
                wait_full(act, l, name)
                act.activation(dst, src, kw.pop("func", ACT.Copy), **kw).then_inc(emptied(name), 1)

            act.wait_ge(x_in, 16 * (KD + 1))
            for k in range(KD - 1):
                chunk(None, 0, k, next_weight(None, k), lambda: None)
            with act.Fori(0, DEPTH) as l:
                hi(l, 0, mid=0)
                chunk(l, 0, KD - 1, NW[:, bass.ds(l * KD + (KD - 1), 1)], lambda: before_layer(act, l))
                before_layer(act, l)
                hi(l, 1)
                def gates(c):
                    for r, n in ((R[6 * c], "r"), (R[6 * c + 1], "i")):
                        evac(l, f"g{c}{n}", two(r[:, :]), psT(f"g{c}{n}"), func=ACT.Tanh, scale=0.5,
                             bias=RGP[:, (2 if n == "i" else 0) + c:(3 if n == "i" else 1) + c])

                def decay(c):
                    tr, q, tau, a = R[6 * c][:, :], R[2][:, :], R[3][:, :], R[4][:, :]
                    wait(act, "q_ready", l, c + 1)
                    act.activation(tau, q, ACT.Tanh).then_inc(S["tau_ready"][0], 1)
                    act.activation(a, q, ACT.Exp, scale=-1.0).then_inc(S["a_ready"][0], 1)
                    wait_emptied(act, l, f"in{12 + c}")
                    act.activation(tr, Z[:, 12 + c, :], ACT.Square).then_inc(S["gl_sq"][0], 1)

                def gelu_and_root(c):
                    tr, g = R[6 * c][:, :], R[5][:, :]
                    wait(act, "gl_arg", l, c + 1)
                    act.activation(tr, tr, ACT.Tanh, scale=G_C2).then_inc(S["gl_tanh"][0], 1)
                    wait(act, "m_ready", l, c + 1)
                    act.activation(g, g, ACT.Sqrt).then_inc(S["g_ready"][0], 1)

                for u in range(N_IN_U):
                    hi(l, u + 2, tile=f"in{ORDER[u]}")
                    if u == 0:
                        root(l, "n1")
                    if u == 4:
                        wait(act, "lam_abs", l, 1)
                        act.activation(RGP[:, 6:8], RGP[:, 4:6], ACT.Exp, scale=-1.0).then_inc(S["lam_exp"][0], 1)
                        wait(act, "rgp_half", l, 1)
                    if u == 6:
                        gates(0)
                    if u == 7:
                        gates(1)
                        squares(l, 0, [Z[:, 0, :]], lambda k: wait_emptied(act, l, "in0"))
                        squares(l, 1, [Z[:, 1, :], Z[:, 2, :]], lambda k: wait_emptied(act, l, f"in{k + 1}"))
                        decay(0)
                    if u == 8:
                        gelu_and_root(0)
                    if u == 9:
                        root(l, "nckv", ACC)
                    if u == 10:
                        decay(1)
                    if u == 11:
                        root(l, "ncq", ACC)
                    if u == 12:
                        gelu_and_root(1)
                wait_full(act, l, "q8")
                for i in range(2):
                    act.activation(QS[0:64, :, :].rearrange("p (a i) b -> p a i b", i=2)[:, :, i, :],
                                   ps("q8")[64 * i:64 * i + 64, 0, 0:4 * NB].rearrange("p (a b) -> p a b", b=NB), ACT.Copy)
                act.activation(Q8[:, :, :], ps("q8")[:, 0, 4 * NB:6 * NB].rearrange("p (a b) -> p a b", b=NB), ACT.Copy)\
                    .then_inc(emptied("q8"), 1)
                for i in range(4):
                    wait(act, "qs_ready", l, 4)
                    plain(act)
                    act.activation(QRB[32 * i:32 * i + 32, :, i, :], QS[64:96, :, :].rearrange("p h b -> p b h"),
                                   ACT.Copy).then_inc(S["qrb_ready"][0], 1)
                evac(l, "ql", QL[:, :, :], ps("ql")[:, 0, 0:64].rearrange("p (h b) -> p b h", h=MH))
                for i in range(2):
                    wait_full(act, l, f"rt{i}")
                    wait(act, "kw_ready", l, 2 * i + 2)
                    act.activation(VT[:, 2 * i:2 * i + 2, :], ps(f"rt{i}")[:, :, 0:256], ACT.Copy)\
                        .then_inc(emptied(f"rt{i}"), 1)
                wait_full(act, l, "ro")
                for c in range(2):
                    i = act.activation(Z[:, 8 + c, 0:SEQ], ps("ro")[:, c, :], ACT.Copy)
                i.then_inc(emptied("ro"), 1)
                wait_full(act, l, "dk")
                act.activation(C8[:, :], ps("dk")[0:NB, 1, 0:P], ACT.Copy)
                act.activation(K8V8[:, :], ps("dk")[0:NB, 0, :], ACT.Copy).then_inc(emptied("dk"), 1)
                wait_full(act, l, "do")
                for i in range(2):
                    r = slice(64 * i, 64 * i + 64)
                    ins = act.activation(Z[r, 8:10, SEQ:T], ps("do")[r, i, 0:2 * NB].rearrange("p (c b) -> p c b", c=2),
                                         ACT.Copy)
                ins.then_inc(emptied("do"), 1)
                for c in range(2):
                    wait_emptied(act, l, f"in{14 + c}")
                    wait(act, "rg_done", l, 2)
                    act.activation(XF[:, c, :], Z[:, 14 + c, :], ACT.Tanh, scale=0.5).then_inc(S["gt_ready"][0], 1)
                for c in range(2):
                    wait_emptied(act, l, f"gm{c}")
                    square_free(l, 3 + c)
                    act.activation(SQ[:, (3 + c) % 2, :], Z[:, 8 + c, :], ACT.Square).then_inc(S["sq_ready"][0], 1)
                for c in range(2):
                    root(l, f"gv{c}")
                for c in range(2):
                    wait(act, "saved", l, 16 * 10)
                    evac(l, f"qr{c}", QR[:, c, :], ps(f"qr{c}")[:, 0, :])
                for i, name in enumerate(("v01", "v23")):
                    wait(act, "ret_done", l, 2)
                    evac(l, name, V[:, 2 * i:2 * i + 2, :], ps(name)[:, :, :])
                for i in range(4):
                    wait(act, "kr_roped", l, 1)
                    wait_full(act, l, "v23")
                    act.activation(KCs[i // 2][64:96, i % 2, :], Z[0:32, Z_KR, 0:SEQ], ACT.Copy).then_inc(S["kr_copied"][0], 1)
                for h in range(MH + 1):
                    if h < MH:
                        p, s = h // 2, (h // 2) % 2
                        if h % 2 == 0:
                            if p >= 2:
                                wait_full(act, l, f"sB{2 * p - 3}")
                            wait_full(act, l, f"q{p}")
                            plain(act)
                            act.activation(QCs[s][0:64, 0, :], ps(f"q{p}")[0:64, 0, :], ACT.Copy)
                            act.activation(QCs[s][0:64, 1, :], ps(f"q{p}")[64:P, 0, :], ACT.Copy).then_inc(emptied(f"q{p}"), 1)
                            wait_full(act, l, f"k{p}")
                            plain(act)
                            act.activation(KCs[s][0:64, 0, :], ps(f"k{p}")[0:64, 0, :], ACT.Copy)
                            act.activation(KCs[s][0:64, 1, :], ps(f"k{p}")[64:P, 0, :], ACT.Copy).then_inc(emptied(f"k{p}"), 1)
                    if h:
                        g = h - 1
                        if g:
                            wait_full(act, l, f"o{g - 1}")
                        wait_full(act, l, f"tA{g}")
                        act.activation(PTR[:, 0:512], ps(f"tA{g}")[:, 0, :], ACT.Copy)
                        act.activation(PTR[:, 512:896], ps(f"tA{g}")[:, 1, 0:384], ACT.Copy).then_inc(emptied(f"tA{g}"), 1)
                    if h < MH:
                        wait(act, "nmax_ready", l, h + 1)
                        if h:
                            wait_full(act, l, f"tB{h - 1}")
                        for q in range(4):
                            o = 128 * (q * (q + 1) // 2)
                            n = f"s{'AB'[q // 2]}{h}"
                            i = act.activation(PR[:, o:o + 128 * (q + 1)], ps(n)[:, q % 2, 0:128 * (q + 1)], ACT.Exp,
                                               scale=SCALE, bias=STAT[:, q:q + 1], accum_out=STAT[:, 8 + q:9 + q])
                            if q % 2:
                                i.then_inc(emptied(n), 1)
                    if "db" in DECODE_TILES[h]:
                        wait(act, "pd_sub", l, 1)
                        act.activation(PD[:, :], PD[:, :], ACT.Exp, scale=SCALE).then_inc(S["pd_ready"][0], 1)
                        act.activation(SMALL[0:NB, 1, :], SMALL[0:NB, 1, :], ACT.Exp, scale=SCALE).then_inc(S["pd_ready"][0], 1)
                    for src, dst in MIX_ROWS.get(h, ()):
                        wait_full(act, l, f"sB{5 if h < MH else 7}")
                        wait(act, "ret_done", l, 2)
                        act.activation(XNH[:, dst, :], Z[:, src, :], ACT.Copy, scale=0.5).then_inc(S["mixr_hi"][0], 1)
                    if h:
                        wait_full(act, l, f"o{g}")
                        r = slice(64 * (g % 2), 64 * (g % 2) + 64)
                        act.activation(XNH[r, 2 + g // 2, 0:SEQ], ps(f"o{g}")[r, 0, :], ACT.Copy).then_inc(S["mix_hi"][0], 1)
                wait_full(act, l, "dy")
                act.activation(XNH[:, 2:6, SEQ:T], ps("dy")[:, 0, 0:4 * NB].rearrange("p (c b) -> p c b", c=4),
                               ACT.Copy).then_inc(S["mix_hi"][0], 1)
                with act.Fori(0, KD // 4) as it:
                    wait_full(act, l, "gv1")
                    for j in range(4):
                        i = TILE_AT["wo0"] + j
                        act.wait_ge(emptied_s[i % 4], l * NT4 + it + (i // 4 + 1 + CREDIT))
                        wait(act, "xsq_added", l, it * 4 + (KD + j - 1))
                        plain(act)
                        act.activation(SQ[:, j % 2:j % 2 + 1, :], X[:, bass.ds(it * 4 + j, 1), :], ACT.Square)\
                            .then_inc(S["xsq_ready"][0], 1)
                        hi(l, U_OUT + j + 2, it, tile=f"wo{j}")
                for k in range(KD):
                    wait_full(act, l, f"wo{KD - 1}")
                    act.activation(XNH[:, k, :], X[:, k, :], ACT.Copy, scale=par("n2", k, k + 1)).then_inc(S["xh_ready"][0], 1)
                root(l, "n2")
                wait(act, "saved", l, 16 * 10)
                act.activation(GB[:, 0, 0:2], const("zero", cols=(0, 2)), ACT.Copy)
                act.activation(GB[:, 1, 0:2], const("zero", cols=(0, 2)), ACT.Copy).then_inc(S["ffn_free"][0], 1)
                for hf, (j0, n) in enumerate(HALVES):
                    t0 = TILE_AT[f"up{hf}_0"]
                    with act.Fori(0, n // 2) as it:
                        for jj in range(2):
                            vi = t0 + 2 * jj + 1
                            c = it * 2 + (j0 + jj)
                            col = it * 2 + (PAR_AT["fcw"][0] + j0 + jj)
                            hi(l, U_UP[hf] + 2 * jj + 2, it, tile=f"up{hf}_{2 * jj}")
                            gi = t0 + 2 * jj
                            act.wait_ge(emptied_s[gi % 4], l * NT4 + it + (gi // 4 + 1 + CREDIT))
                            plain(act)
                            act.activation(YC[:, jj, :], GB[:, jj, 2:T + 2], ACT.Identity,
                                           scale=PAR[:, bass.ds(col + 2 * NJ, 1)], bias=PAR[:, bass.ds(col + 3 * NJ, 1)])\
                                .then_inc(S["y0_ready"][0], 1)
                            wait(act, "yc_ready", l, c + 1)
                            act.activation(TH[:, jj, :], YC[:, jj, :], ACT.Tanh, scale=0.5).then_inc(S["th_ready"][0], 1)
                            hi(l, U_UP[hf] + 2 * jj + 3, it, tile=f"up{hf}_{2 * jj + 1}")
                            act.wait_ge(emptied_s[vi % 4], l * NT4 + it + (vi // 4 + 1 + CREDIT))
                            plain(act)
                            act.activation(HH[:, bass.ds(it * 2 + jj, 1), :], HF[:, jj:jj + 1, :], ACT.Copy)\
                                .then_inc(S["hh_ready"][0], 1)
                    if hf == 0:
                        with act.Fori(0, 2) as it:
                            for j in range(8):
                                hi_down(l, hf, j, it)
                    else:
                        for k in range(KD - 1):
                            hi_down(l, hf, 2 * k)
                            hi_down(l, hf, 2 * k + 1)
                            chunk(l, 2 * KD, k, next_weight(l, k), lambda: wait_emptied(act, l, f"dn1_{k}"))
            before_layer(act, DEPTH)
            wait(act, "xsq_added", DEPTH, KD - 2)
            act.activation(SQ[:, (KD - 1) % 2, :], X[:, KD - 1, :], ACT.Square).then_inc(S["xsq_ready"][0], 1)
            root(DEPTH, "n1")

        @block.vector
        def _(dve):
            V_ = nc.vector
            links = [0]
            D_LINKS = DVE_LINKS
            lay = [0]

            def link(ins):
                links[0] += 1
                ins.then_inc(dve_chain, 1)
                dve.wait_ge(dve_chain, lay[0] * D_LINKS + links[0])

            def lo(l, u, it=None, per=0):
                a = l * (N_UNITS // NHL) + u // NHL + 1
                if it is not None:
                    a = a + it * (per // NHL)
                dve.wait_ge(hi_split[u % NHL], a)
                V_.tensor_tensor(WL[:, u % NHL, :], RAW[:, u % NRAW, :], WH[:, u % NHL, :].bitcast(F32), ALU.subtract)\
                    .then_inc(lo_split[u % NHL], 1)

            def variance(l, name, n, rs=RS[:, :]):
                wait_full(dve, l, name)
                V_.tensor_scalar(two(rs), psT(name), 1.0 / n, EPS, ALU.mult, ALU.add).then_inc(emptied(name), 1)

            def chunk(l, c0, k, weight):
                wait(dve, "xsq_ready", l, c0 + k + 1)
                if k == 0:
                    V_.tensor_copy(ACC, SQ[:, 0, :]).then_inc(S["xsq_added"][0], 1)
                else:
                    wait(dve, "xsq_added", l, c0 + k)
                    V_.tensor_tensor(ACC, ACC, SQ[:, k % 2, :], ALU.add).then_inc(S["xsq_added"][0], 1)
                remainder(l, c0, k, weight)

            def remainder(l, c0, k, weight):
                wait(dve, "xh_ready", l, c0 + k + 1)
                V_.scalar_tensor_tensor(XNL[:, k, :], X[:, k, :], weight, XNH[:, k, :].bitcast(F32), ALU.mult, ALU.subtract)\
                    .then_inc(S["xl_ready"][0], 1)

            def deviation(l, std_no, rs=RS[:, :]):
                wait(dve, "std_ready", l, std_no)
                link(V_.reciprocal(rs, rs))

            def rope(l, name, z, rows, cs, sn, former, done):
                wait_full(dve, l, name)
                wait(dve, former[0], l, former[1])
                V_.tensor_tensor(two(XF[rows, 0, :]), psT(name, rows), two(const(sn, rows)), ALU.mult).then_inc(emptied(name), 1)
                link(V_.tensor_tensor(z, z, const(cs, rows), ALU.mult))
                wait_emptied(dve, l, name)
                V_.tensor_tensor(z, z, XF[rows, 0, :], ALU.add).then_inc(S[done][0], 1)

            dve.wait_ge(pt_in, 16)
            V_.tensor_scalar(PT_SB[:, :], PT_SB[:, :], 0, N_PHYS - 1, ALU.max, ALU.min).then_inc(pt_clamped, 1)
            V_.memset(QRB[:, :, :, :], 0.0)
            V_.memset(STAT[:, :], 0.0)
            dve.sem_inc(S["hl_ready"][0], 1 + CREDIT)
            dve.wait_ge(x_in, 16 * (KD + 1))
            for k in range(KD - 1):
                chunk(None, 0, k, NW[:, k:k + 1])
            with dve.Fori(0, DEPTH) as l:
                lay[0] = l
                links[0] = 0
                dve.wait_ge(tables_in, 16)
                lo(l, 0)
                chunk(l, 0, KD - 1, NW[:, bass.ds(l * KD + (KD - 1), 1)])
                lo(l, 1)
                dve.wait_ge(pars_in, l * 16 + 16)
                V_.memset(GXB[:, :, 0:3], 0.0).then_inc(S["zeroed"][0], 1)
                V_.tensor_scalar(RGP[:, 0:4], par("ba", 0, 4), 0.5, None, ALU.mult).then_inc(S["rgp_half"][0], 1)
                link(V_.tensor_scalar(RGP[:, 8:10], par("lam"), -1.0, None, ALU.mult))
                V_.tensor_tensor(RGP[:, 4:6], RGP[:, 8:10], par("lam"), ALU.max).then_inc(S["lam_abs"][0], 1)
                variance(l, "n1", D_MODEL)
                def rg_constants():
                    s2, e_, pp = RGP[:, 10:12], RGP[:, 6:8], RGP[:, 12:14]
                    s_ = RGP[:, 14:16]
                    wait(dve, "lam_exp", l, 1)
                    link(V_.tensor_scalar(s_, e_, 2.0, None, ALU.add))
                    link(V_.reciprocal(s_, s_))
                    link(V_.tensor_tensor(s_, s_, e_, ALU.mult))
                    link(V_.tensor_tensor(s2, s_, s_, ALU.mult))
                    link(V_.tensor_scalar(pp, s2, 1.0 / 21, None, ALU.mult))
                    for k in range(9, 0, -1):
                        link(V_.scalar_tensor_tensor(pp, pp, 1.0 / (2 * k + 1), s2, ALU.add, ALU.mult))
                    link(V_.scalar_tensor_tensor(pp, pp, 1.0, s_, ALU.add, ALU.mult))
                    link(V_.tensor_scalar(RGP[:, 8:10], RGP[:, 8:10], 0.0, 4.0, ALU.max, ALU.mult))
                    link(V_.scalar_tensor_tensor(RGP[:, 16:18], pp, 8.0, RGP[:, 8:10], ALU.mult, ALU.add))

                def rg_conv(c):
                    xc = Z[:, 10 + c, :]
                    w = lambda k: par("rcw", 4 * c + k, 4 * c + k + 1)
                    wait_emptied(dve, l, f"in{10 + c}")
                    wait(dve, "zeroed", l, 1)
                    link(V_.tensor_scalar(xc, GXB[:, c, 3:T + 3], w(3), par("rcb", c, c + 1), ALU.mult, ALU.add))
                    for k in range(RGC - 1):
                        link(V_.scalar_tensor_tensor(xc[:, 0:SEQ], GXB[:, c, k:k + SEQ], w(k), xc[:, 0:SEQ], ALU.mult, ALU.add))
                        i = V_.scalar_tensor_tensor(xc[:, SEQ:T], par("cbuf", 24 * c + 8 * k, 24 * c + 8 * k + 8), w(k),
                                                    xc[:, SEQ:T], ALU.mult, ALU.add)
                        if k < RGC - 2:
                            link(i)
                        else:
                            i.then_inc(S["conv_done"][0], 1)

                def rg_q(c):
                    wait_emptied(dve, l, f"g{c}r")
                    sp4 = RGP[:, 16 + c:17 + c]
                    V_.tensor_scalar(R[2][:, :], R[6 * c][:, :], sp4, sp4, ALU.mult, ALU.add).then_inc(S["q_ready"][0], 1)

                def rg_middle(c):
                    tr, ti, q, tau, a, g = R[6 * c][:, :], R[6 * c + 1][:, :], *(R[i][:, :] for i in range(2, 6))
                    sp4, gg, xc = RGP[:, 16 + c:17 + c], Z[:, 12 + c, :], Z[:, 10 + c, :]
                    wait(dve, "tau_ready", l, c + 1)
                    link(V_.tensor_scalar(g, tau, 1.0, None, ALU.add))
                    link(V_.reciprocal(g, g))
                    V_.scalar_tensor_tensor(g, tau, 2.0, g, ALU.mult, ALU.mult).then_inc(S["m_ready"][0], 1)
                    wait(dve, "gl_sq", l, c + 1)
                    link(V_.tensor_scalar(tr, tr, G_C1, 1.0, ALU.mult, ALU.add))
                    V_.tensor_tensor(tr, tr, gg, ALU.mult).then_inc(S["gl_arg"][0], 1)
                    wait_emptied(dve, l, f"g{c}i")
                    link(V_.scalar_tensor_tensor(ti, ti, 1.0, xc, ALU.add, ALU.mult))

                def rg_scan(c):
                    tr, ti, q, tau, a, g = R[6 * c][:, :], R[6 * c + 1][:, :], *(R[i][:, :] for i in range(2, 6))
                    sp4, gg, xc = RGP[:, 16 + c:17 + c], Z[:, 12 + c, :], Z[:, 10 + c, :]
                    wait(dve, "g_ready", l, c + 1)
                    link(V_.scalar_tensor_tensor(ti, ti, 0.5, g, ALU.mult, ALU.mult))
                    wait(dve, "a_ready", l, c + 1)
                    link(V_.tensor_tensor_scan(xc[:, 0:SEQ], a[:, 0:SEQ], ti[:, 0:SEQ], 0.0, ALU.mult, ALU.add))
                    link(V_.tensor_tensor(q[:, 0:NB], a[:, SEQ:T], par("h0", 8 * c, 8 * c + 8), ALU.mult))
                    link(V_.tensor_tensor(xc[:, SEQ:T], q[:, 0:NB], ti[:, SEQ:T], ALU.add))
                    wait(dve, "gl_tanh", l, c + 1)
                    link(V_.scalar_tensor_tensor(gg, tr, 1.0, gg, ALU.add, ALU.mult))
                    V_.tensor_tensor(gg, gg, xc, ALU.mult).then_inc(S["rg_done"][0], 1)

                for u in range(2, N_IN_U + 2):
                    lo(l, u)
                    v = ORDER[u - 2]
                    if u == 2:
                        deviation(l, 1)
                    r = slice(0, 32) if v == Z_KR else slice(0, P)
                    dst = GXB[:, v - 10, 3:T + 3] if v in Z_GX else Z[r, v, :]
                    wait_full(dve, l, f"in{v}")
                    V_.scalar_tensor_tensor(two(dst), psT(f"in{v}", r), 0.125 if v in Z_RK else 1.0, two(RS[r, :]),
                                            ALU.mult, ALU.mult).then_inc(emptied(f"in{v}"), 1)
                    if u == 10:
                        variance(l, "nckv", KVR, ACC)
                    if u == 12:
                        deviation(l, 2, ACC)
                        V_.scalar_tensor_tensor(Z[:, 0, :], Z[:, 0, :], par("kn"), ACC, ALU.mult, ALU.mult)\
                            .then_inc(S["cq_normed"][0], 1)
                        wait(dve, "cq_normed", l, 1)
                        variance(l, "ncq", QR_, ACC)
                    if u == 14:
                        deviation(l, 3, ACC)
                        for k in range(2):
                            V_.scalar_tensor_tensor(Z[:, 1 + k, :], Z[:, 1 + k, :], par("qn", k, k + 1), ACC,
                                                    ALU.mult, ALU.mult).then_inc(S["cq_normed"][0], 1)
                    if u == 5:
                        rg_conv(0)
                    if u == 6:
                        rg_conv(1)
                    if u == 7:
                        rg_constants()
                    if u == 8:
                        rg_q(0)
                    if u == 9:
                        rg_middle(0)
                    if u == 11:
                        rg_scan(0)
                    if u == 12:
                        rg_q(1)
                    if u == 13:
                        rg_middle(1)
                    if u == 15:
                        rg_scan(1)
                rope(l, "pkr", Z[0:32, Z_KR, :], slice(0, 32), "cosm", "sinm", ("xl_ready", KD), "kr_roped")
                for i, z in enumerate((3, 5, 6, 7)):
                    rope(l, f"pz{i}", Z[:, z, :], slice(0, P), "cosr", "sinr", ("roped", i) if i else ("kr_roped", 1), "roped")
                cs = lambda n: const(n, cols=(SEQ, T)).rearrange("p (a b) -> p a b", a=1).broadcast_to([P, 2, NB])
                pq = ps("pq8")[:, 0, 0:2 * NB].rearrange("p (a b) -> p a b", b=NB)
                wait_full(dve, l, "pq8")
                V_.tensor_tensor(pq, pq, cs("sinm"), ALU.mult)
                link(V_.tensor_tensor(Q8[:, :, :], Q8[:, :, :], cs("cosm"), ALU.mult))
                V_.tensor_tensor(Q8[:, :, :], Q8[:, :, :], pq, ALU.add).then_inc(emptied("pq8"), 1)
                wait_emptied(dve, l, "pq8")
                for i in range(4):
                    V_.tensor_copy(QS[64:96, :, :].rearrange("p (a i) b -> p a i b", i=4)[:, :, i, :],
                                   Q8[32 * i:32 * i + 32, :, :]).then_inc(S["qs_ready"][0], 1)
                SN, PN, M1, MB, RSUM, RD, OL = (SMALL[:, i, :] for i in range(7))

                def page_scores(b):
                    wait_full(dve, l, f"ds{b}")
                    dve.sem_inc(pages_used[b % 2], 1)
                    rings_split(dve, l, N_IN_U)
                    rings_split(dve, l, N_IN_U + 1)
                    n = N_PAGES * MH
                    V_.tensor_copy(PD[:, n * b:n * b + n], ps(f"ds{b}")[:, 0, 0:n])
                    V_.tensor_reduce(M1[:, MH * b:MH * b + MH], ps(f"ds{b}")[:, 0, 0:n].rearrange("p (j h) -> p h j", h=MH),
                                     AX, ALU.max).then_inc(emptied(f"ds{b}"), 1)

                page_scores(0)
                page_scores(1)
                for c in range(2):
                    gq = const("gq", cols=(P * c, P * c + P)).rearrange("p (a t) -> p a t", a=1).broadcast_to([P, 4, P])
                    wait(dve, "roped", l, 4)
                    V_.tensor_tensor(QD[:, c, :].rearrange("p (a t) -> p a t", a=4),
                                     Z[:, (3, 5)[c], 0:SEQ].rearrange("p (a t) -> p a t", a=4), gq, ALU.mult)\
                        .then_inc(S["qd_ready"][0], 1)
                for n in range(4):
                    wait_full(dve, l, f"rt{n // 2}")
                    V_.tensor_tensor(KW[:, n, :], ps(f"rt{n // 2}")[:, n % 2, 256:512], const("wk"), ALU.mult)\
                        .then_inc(S["kw_ready"][0], 1)
                for n in range(4):
                    t = f"rs{n // 2}"
                    wait_full(dve, l, t)
                    i = V_.tensor_tensor(two(SM[:, n, :]), ps(t)[:, :, 256 * (n % 2):256 * (n % 2) + 256],
                                         two(const("decay")), ALU.mult)
                    if n % 2:
                        i.then_inc(emptied(t), 1)
                wait_full(dve, l, "kv")
                link(V_.tensor_copy(SS[:, 0, :], ps("kv")[:, 0, 0:P]))
                for n in range(1, 4):
                    for c in range(2):
                        i = V_.scalar_tensor_tensor(SS[:, n, HD * c:HD * c + HD], SS[:, n - 1, HD * c:HD * c + HD],
                                                    const("gam", cols=(c, c + 1)),
                                                    ps("kv")[:, 0, P * n + HD * c:P * n + HD * c + HD], ALU.mult, ALU.add)
                        if (n, c) == (3, 1):
                            i.then_inc(emptied("kv"), 1)
                        elif c:
                            link(i)
                page_scores(2)
                wait_emptied(dve, l, "dk")
                for h in range(RH):
                    v8 = K8V8[:, 256 + HD * h:256 + HD * h + HD].rearrange("p (a e) -> p a e", a=1).broadcast_to([NB, NB, HD])
                    V_.tensor_tensor(VM[:, h, :].rearrange("p (b e) -> p b e", b=NB), v8,
                                     const("bmask", slice(0, NB)).rearrange("p (b e) -> p b e", b=NB), ALU.mult)\
                        .then_inc(S["vm_ready"][0], 1)
                wait_full(dve, l, "du")
                dve.wait_ge(sd_in, l * 16 + 16)
                for c in range(2):
                    i = V_.scalar_tensor_tensor(SD[:, c, :], SD[:, c, :], const("gam", cols=(2 + c, 3 + c)),
                                                ps("du")[:, c, :], ALU.mult, ALU.add)
                i.then_inc(emptied("du"), 1)
                page_scores(3)
                for c in range(2):
                    wait_full(dve, l, f"gm{c}")
                    V_.tensor_tensor(two(Z[:, 8 + c, :]), two(Z[:, 8 + c, :]), psT(f"gm{c}"), ALU.subtract).then_inc(emptied(f"gm{c}"), 1)
                for c in range(2):
                    wait(dve, "gt_ready", l, c + 1)
                    V_.scalar_tensor_tensor(Z[:, 14 + c, :], XF[:, c, :], 1.0, Z[:, 14 + c, :], ALU.add, ALU.mult)\
                        .then_inc(S["gt_silu"][0], 1)
                for c in range(2):
                    variance(l, f"gv{c}", 1.0)
                    deviation(l, 4 + c)
                    link(V_.scalar_tensor_tensor(Z[:, 8 + c, :], Z[:, 8 + c, :], par("gn", c, c + 1), RS[:, :], ALU.mult, ALU.mult))
                    V_.tensor_tensor(Z[:, 8 + c, :], Z[:, 8 + c, :], Z[:, 14 + c, :], ALU.mult).then_inc(S["ret_done"][0], 1)
                page_scores(4)
                wait(dve, "ret_done", l, 2)
                for c in range(2):
                    wait_emptied(dve, l, f"qr{c}")
                    wait_full(dve, l, f"pqr{c}")
                    wait(dve, *(("roped", l, 5) if c else ("gt_silu", l, 2)))
                    V_.tensor_tensor(XF[:, 0, 0:SEQ], ps(f"pqr{c}")[:, 0, :], const("sinm", cols=(0, SEQ)), ALU.mult)\
                        .then_inc(emptied(f"pqr{c}"), 1)
                    link(V_.tensor_tensor(QR[:, c, :], QR[:, c, :], const("cosm", cols=(0, SEQ)), ALU.mult))
                    wait_emptied(dve, l, f"pqr{c}")
                    V_.tensor_tensor(QR[:, c, :], QR[:, c, :], XF[:, 0, 0:SEQ], ALU.add).then_inc(S["roped"][0], 1)
                page_scores(5)
                wait(dve, "roped", l, 6)
                for h in range(MH + 1):
                    if h < MH:
                        p, s = h // 2, (h // 2) % 2
                        if h % 2 == 0:
                            for i in range(2):
                                wait_full(dve, l, f"q{p}")
                                r = 32 * ((2 * p + i) % 4)
                                V_.tensor_copy(QCs[s][64:96, i, :], QR[r:r + 32, p // 2, :]).then_inc(S["qk_ready"][0], 1)
                        for q in range(4):
                            n = f"s{'AB'[q // 2]}{h}"
                            if q % 2 == 0:
                                wait_full(dve, l, n)
                            dg = ps(n)[:, q % 2, 128 * q:128 * q + 128]
                            i = V_.tensor_tensor(dg, dg, const("causal"), ALU.add)
                        link(i)
                        for q in range(4):
                            n = f"s{'AB'[q // 2]}{h}"
                            i = V_.tensor_reduce(STAT[:, 4 + q:5 + q], ps(n)[:, q % 2, 0:128 * (q + 1)], AX, ALU.max)
                        link(i)
                        V_.tensor_scalar(STAT[:, 0:4], STAT[:, 4:8], -SCALE, None, ALU.mult).then_inc(S["nmax_ready"][0], 1)
                    if h:
                        g = h - 1
                        if g:
                            wait_full(dve, l, f"o{g - 1}")
                        wait_full(dve, l, f"tB{g}")
                        V_.tensor_copy(PTR[:, 896:1152], ps(f"tB{g}")[:, 0, 0:256])
                        V_.tensor_copy(PTR[:, 1152:1280], ps(f"tB{g}")[:, 1, 0:128]).then_inc(emptied(f"tB{g}"), 1)
                    if h < MH:
                        wait_emptied(dve, l, f"sA{h}")
                        wait_emptied(dve, l, f"sB{h}")
                        link(V_.reciprocal(STAT[:, 12:16], STAT[:, 8:12]))
                        for q in range(4):
                            o = 128 * (q * (q + 1) // 2)
                            i = V_.tensor_scalar(PR[:, o:o + 128 * (q + 1)], PR[:, o:o + 128 * (q + 1)],
                                                 STAT[:, 12 + q:13 + q], None, ALU.mult)
                        i.then_inc(S["p_ready"][0], 1)
                    def decode_step(name):
                        if name != "dy":
                            wait_full(dve, l, name)
                        if name[:2] == "ds":
                            page_scores(int(name[2:]))
                        elif name == "dn":
                            V_.tensor_tensor(SN[0:NB, :], ps("dn")[0:NB, 0, 0:64], const("newmask", slice(0, NB)), ALU.add)\
                                .then_inc(emptied("dn"), 1)
                            wait_emptied(dve, l, "ds7")
                            wait_emptied(dve, l, "dn")
                            V_.tensor_tensor(M1[0:NB, :], M1[0:NB, :], SN[0:NB, :], ALU.max).then_inc(S["m_all"][0], 1)
                        elif name == "dm":
                            link(V_.tensor_reduce(SMALL[0:64, 8, 0:1], ps("dm")[0:64, 0, 0:P], AX, ALU.max))
                            V_.tensor_scalar(SMALL[0:64, 7, :], const("ident", slice(0, 64), (0, 64)), SMALL[0:64, 8, 0:1],
                                             None, ALU.mult).then_inc(emptied("dm"), 1)
                        elif name == "db":
                            V_.tensor_copy(MB, ps("db")[:, 0, 0:64]).then_inc(emptied("db"), 1)
                            wait_emptied(dve, l, "db")
                            V_.tensor_tensor(PN[0:NB, :], SN[0:NB, :], MB[0:NB, :], ALU.subtract).then_inc(S["sn_sub"][0], 1)
                            for a in range(2):
                                pd = PD[:, 512 * a:512 * a + 512].rearrange("p (b j h) -> p b j h", b=4, j=N_PAGES)
                                mb = MB[:, 32 * a:32 * a + 32].rearrange("p (b o h) -> p b o h", b=4, o=1)
                                i = V_.tensor_tensor(pd, pd, mb.broadcast_to([P, 4, N_PAGES, MH]), ALU.subtract)
                            i.then_inc(S["pd_sub"][0], 1)
                            wait(dve, "pd_ready", l, 1)
                            link(V_.tensor_reduce(RSUM.rearrange("p (b h) -> p b h", b=NB),
                                                  PD[:, :].rearrange("p (b j h) -> p b h j", b=NB, j=N_PAGES), AX, ALU.add))
                            wait(dve, "pd_ready", l, 2)
                            V_.tensor_tensor(RSUM[0:NB, :], RSUM[0:NB, :], PN[0:NB, :], ALU.add).then_inc(S["rsum_ready"][0], 1)
                        elif name == "dd":
                            V_.reciprocal(RD, ps("dd")[:, 0, 0:64]).then_inc(emptied("dd"), 1)
                        elif name[:2] == "dp":
                            b = int(name[2:])
                            dve.sem_inc(pages_used[b % 2], 1)
                            V_.tensor_copy(O8[:, P * b:P * b + P], ps(name)[0:MH, 0, 0:P]).then_inc(emptied(name), 1)
                        else:
                            wait_emptied(dve, l, "dd")
                            wait(dve, "ot_ready", l, 1)
                            V_.tensor_tensor(OL, ps("dy")[:, 1, 0:64], RD, ALU.mult).then_inc(S["ol_ready"][0], 1)

                    for name in DECODE_TILES[h]:
                        decode_step(name)
                    for i, (src, dst) in enumerate(MIX_ROWS.get(h, ())):
                        wait(dve, "mixr_hi", l, 2 * (h - MH + 1) + i + 1)
                        V_.scalar_tensor_tensor(XNL[:, dst, :], Z[:, src, :], 0.5, XNH[:, dst, :].bitcast(F32),
                                                ALU.mult, ALU.subtract).then_inc(S["mix_lo"][0], 1)
                    if h:
                        g = h - 1
                        r = slice(64 * (g % 2), 64 * (g % 2) + 64)
                        wait(dve, "mix_hi", l, g + 1)
                        V_.tensor_tensor(XNL[r, 2 + g // 2, 0:SEQ], ps(f"o{g}")[r, 0, :], XNH[r, 2 + g // 2, 0:SEQ].bitcast(F32),
                                         ALU.subtract).then_inc(emptied(f"o{g}"), 1)
                wait(dve, "mix_hi", l, 9)
                V_.tensor_tensor(XNL[:, 2:6, SEQ:T], ps("dy")[:, 0, 0:4 * NB].rearrange("p (c b) -> p c b", c=4),
                                 XNH[:, 2:6, SEQ:T].bitcast(F32), ALU.subtract).then_inc(emptied("dy"), 1)
                t0 = TILE_AT["wo0"]
                wait(dve, "roped", l, 6)
                V_.memset(ACC, 0.0).then_inc(S["acc_zero"][0], 1)
                with dve.Fori(0, KD // 4) as it:
                    wait(dve, "acc_zero", l, 1)
                    for j in range(4):
                        i = t0 + j
                        dve.wait_ge(full_s[i % 4], l * NT4 + it + (i // 4 + 1))
                        xm = X[:, bass.ds(it * 4 + j, 1), :].rearrange("p a (b n) -> p (a b) n", b=2)
                        V_.tensor_tensor(xm, xm, PS[i % 4][:, :, 0:HB], ALU.add).then_inc(emptied_s[i % 4], 1)
                        wait(dve, "xsq_ready", l, it * 4 + (KD + j + 1))
                        wait(dve, "xsq_added", l, it * 4 + (KD + j))
                        V_.tensor_tensor(XF[:, 1:2, :], XF[:, 1:2, :], SQ[:, j % 2:j % 2 + 1, :], ALU.add)\
                            .then_inc(S["xsq_added"][0], 1)
                        lo(l, U_OUT + j + 2, it, 4)
                for k in range(KD):
                    remainder(l, KD, k, par("n2", k, k + 1))
                variance(l, "n2", D_MODEL)
                deviation(l, 6)
                wait(dve, "ffn_free", l, 1)
                settle(dve)
                for hf, (j0, n) in enumerate(HALVES):
                    t0 = TILE_AT[f"up{hf}_0"]
                    with dve.Fori(0, n // 2) as it:
                        for jj in range(2):
                            vi = t0 + 2 * jj + 1
                            c = it * 2 + (j0 + jj)
                            col = it * 2 + (PAR_AT["fcw"][0] + j0 + jj)
                            w = lambda k: PAR[:, bass.ds(col + k * NJ, 1)]
                            fb = lambda k: PAR[:, bass.ds(it * 32 + (PAR_AT["fbuf"][0] + 16 * (j0 + jj) + 8 * k), NB)]
                            y = YC[:, jj, :]
                            gi = t0 + 2 * jj
                            wait(dve, "hl_ready", l, c)
                            dve.wait_ge(full_s[gi % 4], l * NT4 + it + (gi // 4 + 1))
                            V_.tensor_tensor(two(GB[:, jj, 2:T + 2]), PS[gi % 4][:, :, 0:HB], two(RS[:, :]), ALU.mult)\
                                .then_inc(emptied_s[gi % 4], 1)
                            dve.wait_ge(emptied_s[gi % 4], l * NT4 + it + (gi // 4 + 1 + CREDIT))
                            V_.tensor_copy(FOUT[:, bass.ds(c, 1), :].rearrange("p a n -> p (a n)"), GB[:, jj, SEQ:T + 2])\
                                .then_inc(S["fout_ready"][0], 1)
                            wait(dve, "y0_ready", l, c + 1)
                            for k in (1, 0):
                                V_.scalar_tensor_tensor(y[:, SEQ:T], fb(k), w(k), y[:, SEQ:T], ALU.mult, ALU.add)\
                                    .then_inc(S["conv_step"][0], 1)
                                i = V_.scalar_tensor_tensor(y[:, 0:SEQ], GB[:, jj, k:k + SEQ], w(k), y[:, 0:SEQ], ALU.mult, ALU.add)
                                if k:
                                    i.then_inc(S["conv_step"][0], 1)
                                    dve.wait_ge(S["conv_step"][0], l * (3 * NJ) + c * 3 + 2)
                                else:
                                    i.then_inc(S["yc_ready"][0], 1)
                            lo(l, U_UP[hf] + 2 * jj + 2, it, 4)
                            wait(dve, "yc_ready", l, c + 1)
                            V_.tensor_tensor(HF[:, jj, :], y, RS[:, :], ALU.mult).then_inc(S["yr_ready"][0], 1)
                            wait(dve, "th_ready", l, c + 1)
                            wait(dve, "yr_ready", l, c + 1)
                            V_.scalar_tensor_tensor(TH[:, jj, :], TH[:, jj, :], 1.0, HF[:, jj, :], ALU.add, ALU.mult)\
                                .then_inc(S["hf_ready"][0], 1)
                            wait(dve, "hf_ready", l, c + 1)
                            dve.wait_ge(full_s[vi % 4], l * NT4 + it + (vi // 4 + 1))
                            V_.scalar_tensor_tensor(two(HF[:, jj, :]), two(TH[:, jj, :]), 0.5, PS[vi % 4][:, :, 0:HB],
                                                    ALU.mult, ALU.mult).then_inc(emptied_s[vi % 4], 1)
                            lo(l, U_UP[hf] + 2 * jj + 3, it, 4)
                            wait(dve, "hh_ready", l, c + 1)
                            hsl = bass.ds(it * 2 + jj, 1)
                            V_.tensor_tensor(HL[:, hsl, :], HF[:, jj:jj + 1, :], HH[:, hsl, :].bitcast(F32), ALU.subtract)\
                                .then_inc(S["hl_ready"][0], 1)
                    t0 = TILE_AT[f"dn{hf}_0"]

                    def down(it, split_to):
                        for j in range(4):
                            for x in (2 * j, 2 * j + 1):
                                if x < split_to:
                                    lo(l, U_DN[hf] + x + 2, it, 8)
                            i = t0 + j
                            dve.wait_ge(full_s[i % 4], l * NT4 + it + (i // 4 + 1))
                            m = it * 4 + j
                            xm = X[:, bass.ds(m, 1), :] if not isinstance(m, int) else X[:, m:m + 1, :]
                            xm = xm.rearrange("p a (b n) -> p (a b) n", b=2)
                            V_.tensor_tensor(xm, xm, PS[i % 4][:, :, 0:HB], ALU.add).then_inc(emptied_s[i % 4], 1)
                            if isinstance(m, int) and m < KD - 1:
                                chunk(l, 2 * KD, m, NW[:, bass.ds(l * KD + (KD + m), 1)])

                    if hf == 0:
                        with dve.Fori(0, 2) as it:
                            down(it, 8)
                    else:
                        down(0, 8)
                        down(1, 6)
                assert links[0] == D_LINKS, f"DVE_LINKS is {links[0]}"
            lay[0], links[0] = DEPTH, 0
            wait(dve, "xsq_ready", DEPTH, KD)
            wait(dve, "xsq_added", DEPTH, KD - 1)
            V_.tensor_tensor(ACC, ACC, SQ[:, (KD - 1) % 2, :], ALU.add).then_inc(S["xsq_added"][0], 1)
            variance(DEPTH, "n1", D_MODEL)
            deviation(DEPTH, 1)
            for k in range(KD):
                if k >= 2:
                    dve.wait_ge(y_saved[k % 2], 16 * (k // 2))
                V_.scalar_tensor_tensor(XF[:, k % 2, :], X[:, k, :], NW[:, DEPTH * KD + k:DEPTH * KD + k + 1], RS[:, :],
                                        ALU.mult, ALU.mult).then_inc(S["xf_ready"][0], 1)

        @block.tensor
        def _(pe):
            mm = nc.tensor.matmul

            def product(l, name, us, xh, xl, rows=P, it=None, per=0, norm=None, chunks=None):
                i = TILE_AT[name]
                a = l * NT4 + i // 4 + CREDIT
                pe.wait_ge(emptied_s[i % 4], a if it is None else a + it)
                total = sum(n for _, n in us)
                kk = 0
                for u, n in us:
                    b = l * (N_UNITS // NHL) + u // NHL + 1 + CREDIT
                    pe.wait_ge(lo_split[u % NHL], b if it is None else b + it * (per // NHL))
                    plain(pe)
                    for k in range(n):
                        if chunks is not None and kk == total - 1:
                            wait(pe, "hl_ready", l, chunks + 1)
                            plain(pe)
                        if norm is not None:
                            wait(pe, "xl_ready", l, norm + k + 1)
                            plain(pe)
                        wh = WH[:, u % NHL, k * rows:(k + 1) * rows]
                        wl = WL[:, u % NHL, k * rows:(k + 1) * rows]
                        for s, (w, x) in enumerate(((wh, xh), (wh, xl), (wl, xh))):
                            for hb in range(2):
                                last = mm(PS[i % 4][0:rows, hb, 0:HB], w, x(kk)[:, hb * HB:(hb + 1) * HB],
                                          start=(kk == 0 and s == 0), stop=(kk == total - 1 and s == 2))
                        kk += 1
                    last.then_inc(full_s[i % 4] if kk == total else S["mid_used"][0], 1)

            xh = lambda k: XNH[:, k, :]
            xl = lambda k: XNL[:, k, :]

            def tile(l, name):
                wait_tile(pe, l, name)
                plain(pe)

            def halves(name, lhsT, rhs, rows=slice(0, P), start=True, stop=True):
                for hb in range(2):
                    last = mm(ps(name)[rows, hb, 0:HB], lhsT, rhs[:, hb * HB:(hb + 1) * HB], start=start, stop=stop)
                return last

            def sums(l, name, q0, lhs):
                n = SQ_USES[q0][2]
                tile(l, name)
                for k in range(n):
                    wait(pe, "sq_ready", l, q0 + k + 1)
                    plain(pe)
                    last = halves(name, lhs, SQ[:, (q0 + k) % 2, :], start=(k == 0), stop=(k == n - 1))
                    last.then_inc(full(name) if k == n - 1 else S["sq_used"][0], 1)

            def norm_sum(l, name, c0):
                pe.wait_ge(tables_in, 16)
                tile(l, name)
                wait(pe, "xsq_added", l, c0 + KD)
                plain(pe)
                halves(name, const("ones"), ACC).then_inc(full(name), 1)

            def swap(l, name, perm, src, rows=P):
                tile(l, name)
                halves(name, const(perm, slice(0, rows), (0, rows)), src, slice(0, rows)).then_inc(full(name), 1)

            with pe.Fori(0, DEPTH) as l:
                def gates(c):
                    for g, n in enumerate("ri"):
                        wait_tile(pe, l, f"g{c}{n}")
                        wait(pe, "conv_done", l, c + 1)
                        plain(pe)
                        halves(f"g{c}{n}", WG[:, 2 * g + c, :], Z[:, 10 + c, :]).then_inc(full(f"g{c}{n}"), 1)

                for u in range(N_IN_U):
                    product(l, f"in{ORDER[u]}", [(u, KD)], xh, xl, 32 if u == U_KR else P, norm=None if u else 0)
                    if u == 0:
                        norm_sum(l, "n1", 0)
                    if u == 6:
                        pe.wait_ge(small_in, l * 80 + 80)
                        settle(pe)
                        gates(0)
                    if u == 7:
                        gates(1)
                    if u == 8:
                        sums(l, "nckv", 0, const("ones"))
                        sums(l, "ncq", 1, const("ones"))
                plain(pe)
                wait_emptied(pe, l, "in4")
                swap(l, "pkr", "perm32", Z[0:32, Z_KR, :], 32)
                for i, z in enumerate((3, 5, 6, 7)):
                    wait_emptied(pe, l, f"in{z}")
                    swap(l, f"pz{i}", "perm64", Z[:, z, :])
                pe.wait_ge(small_in, l * 80 + 80)
                wait(pe, "cq_normed", l, 3)
                tile(l, "q8")
                for c in range(6):
                    for k in range(2):
                        last = mm(ps("q8")[:, 0, NB * c:NB * c + NB], UQ[:, k, P * c:P * c + P], Z[:, 1 + k, SEQ:T],
                                  start=(k == 0), stop=(k == 1))
                last.then_inc(full("q8"), 1)
                plain(pe)
                wait_emptied(pe, l, "q8")
                tile(l, "pq8")
                mm(ps("pq8")[:, 0, 0:2 * NB], const("perm32"), Q8[:, :, :].rearrange("p a b -> p (a b)"), start=True, stop=True)\
                    .then_inc(full("pq8"), 1)
                tile(l, "ql")
                for h in range(MH):
                    last = mm(ps("ql")[:, 0, NB * h:NB * h + NB], UKT[:, h, :], QS[0:64, h, :], start=True, stop=True)
                last.then_inc(full("ql"), 1)

                def page_scores(b):
                    s, name = b % 2, f"ds{b}"
                    if b == 0:
                        wait(pe, "qrb_ready", l, 4)
                        wait_emptied(pe, l, "ql")
                        settle(pe)
                    wait_tile(pe, l, name)
                    pe.wait_ge(pages_in[s], l * per_layer + (b // 2 + 1) * 16 * 2 * N_PAGES)
                    plain(pe)
                    for j in range(N_PAGES):
                        o = j * MH
                        if j % 4 == 0:
                            mm(ps(name)[:, 0, o:o + 4 * MH], RT[:, s, P * (j // 4):P * (j // 4) + P],
                               QRB[:, b, :, :].rearrange("p g h -> p (g h)"), start=True, stop=False)
                        last = mm(ps(name)[:, 0, o:o + MH], KT[:, s, P * j:P * j + P], QL[:, b, :],
                                  start=False, stop=j % 4 == 3)
                    last.then_inc(full(name), 1)

                per_layer = 16 * (3 * N_PAGES) * (NB // 2)
                page_scores(0)
                page_scores(1)
                wait(pe, "roped", l, 4)
                wait_emptied(pe, l, "in9")
                idt = const("ident")
                flat = lambda t: t.rearrange("p b h -> p (b h)")
                for n in range(4):
                    t = f"rt{n // 2}"
                    if n % 2 == 0:
                        tile(l, t)
                    for i, z in enumerate((8, 9, 6, 7)):
                        last = nc.tensor.transpose(ps(t)[:, n % 2, P * i:P * i + P], Z[:, z, P * n:P * n + P], idt)
                    if n % 2:
                        last.then_inc(full(t), 1)
                half = lambda h: slice(64 * (h % 2), 64 * (h % 2) + 64)
                for n in range(4):
                    t = f"rs{n // 2}"
                    if n % 2 == 0:
                        tile(l, t)
                    for h in range(RH):
                        o = 256 * (n % 2) + P * (h // 2)
                        last = mm(ps(t)[:, h % 2, o:o + P], Z[half(h), 6 + h // 2, P * n:P * n + P],
                                  Z[half(h), (3, 5)[h // 2], P * n:P * n + P], start=True, stop=True)
                    if n % 2:
                        last.then_inc(full(t), 1)
                wait_emptied(pe, l, "rt1")
                wait(pe, "kw_ready", l, 4)
                tile(l, "kv")
                for n in range(4):
                    for h in range(RH):
                        o = P * n + HD * (h // 2)
                        last = mm(ps("kv")[half(h), 0, o:o + HD], KW[:, n, HD * h:HD * h + HD], VT[:, n, HD * h:HD * h + HD],
                                  start=True, stop=True)
                last.then_inc(full("kv"), 1)
                page_scores(2)
                wait_emptied(pe, l, "rs1")
                wait_emptied(pe, l, "kv")
                wait(pe, "qd_ready", l, 2)
                tile(l, "ro")
                for n in range(4):
                    for h in range(RH):
                        o = 256 * (h % 2) + P * (h // 2)
                        out = ps("ro")[half(h), h // 2, P * n:P * n + P]
                        last = mm(out, VT[:, n, HD * h:HD * h + HD], SM[:, n, o:o + P], start=True, stop=(n == 0))
                        if n:
                            c = h // 2
                            last = mm(out, SS[half(h), n - 1, HD * c:HD * c + HD], QD[half(h), c, P * n:P * n + P],
                                      start=False, stop=True)
                last.then_inc(full("ro"), 1)
                wait(pe, "cq_normed", l, 1)
                tile(l, "dk")
                for i, z in enumerate((6, 7, 8, 9)):
                    nc.tensor.transpose(ps("dk")[0:NB, 0, P * i:P * i + P], Z[:, z, SEQ:T], idt)
                nc.tensor.transpose(ps("dk")[0:NB, 1, 0:P], Z[:, Z_CKV, SEQ:T], idt).then_inc(full("dk"), 1)
                wait(pe, "vm_ready", l, 4)
                wait_emptied(pe, l, "dk")
                tile(l, "du")
                for h in range(RH):
                    last = mm(ps("du")[half(h), h // 2, :], K8V8[:, HD * h:HD * h + HD], VM[:, h, :], start=True, stop=True)
                last.then_inc(full("du"), 1)
                plain(pe)
                wait_emptied(pe, l, "du")
                tile(l, "do")
                for h in range(RH):
                    for b in range(NB):
                        c = h // 2
                        last = mm(ps("do")[half(h), h % 2, NB * c + b:NB * c + b + 1], SD[half(h), c, HD * b:HD * b + HD],
                                  Z[half(h), (3, 5)[c], SEQ + b:SEQ + b + 1], start=True, stop=True)
                last.then_inc(full("do"), 1)
                page_scores(3)
                wait_emptied(pe, l, "ro")
                wait_emptied(pe, l, "do")
                for c in range(2):
                    tile(l, f"gm{c}")
                    halves(f"gm{c}", const("bd64"), Z[:, 8 + c, :]).then_inc(full(f"gm{c}"), 1)
                sums(l, "gv0", 3, const("bd64"))
                sums(l, "gv1", 4, const("bd64"))
                page_scores(4)
                for c in range(2):
                    tile(l, f"qr{c}")
                    for k in range(2):
                        last = mm(ps(f"qr{c}")[:, 0, :], UQ[:, k, 512 + P * c:512 + P * c + P], Z[:, 1 + k, 0:SEQ],
                                  start=(k == 0), stop=(k == 1))
                    last.then_inc(full(f"qr{c}"), 1)
                    wait_emptied(pe, l, f"qr{c}")
                    tile(l, f"pqr{c}")
                    mm(ps(f"pqr{c}")[:, 0, :], const("perm32"), QR[:, c, :], start=True, stop=True).then_inc(full(f"pqr{c}"), 1)
                page_scores(5)
                for n in range(4):
                    t = ("v01", "v23")[n // 2]
                    if n % 2 == 0:
                        tile(l, t)
                    last = mm(ps(t)[:, n % 2, :], Z[:, Z_CKV, P * n:P * n + P], UV[:, :], start=True, stop=True)
                    if n % 2:
                        last.then_inc(full(t), 1)
                wait(pe, "kr_copied", l, 4)
                off = (0, 512, 896, 1152)
                for h in range(MH + 1):
                    if h < MH:
                        p, s = h // 2, (h // 2) % 2
                        if h % 2 == 0:
                            tile(l, f"q{p}")
                            for k in range(2):
                                last = mm(ps(f"q{p}")[:, 0, :], UQ[:, k, P * p:P * p + P], Z[:, 1 + k, 0:SEQ],
                                          start=(k == 0), stop=(k == 1))
                            last.then_inc(full(f"q{p}"), 1)
                            tile(l, f"k{p}")
                            mm(ps(f"k{p}")[:, 0, :], UK[:, P * p:P * p + P], Z[:, Z_CKV, 0:SEQ], start=True, stop=True)\
                                .then_inc(full(f"k{p}"), 1)
                            plain(pe)
                            wait_emptied(pe, l, f"q{p}")
                            wait_emptied(pe, l, f"k{p}")
                            wait(pe, "qk_ready", l, 2 * p + 2)
                        for q in range(4):
                            n = f"s{'AB'[q // 2]}{h}"
                            if q % 2 == 0:
                                tile(l, n)
                            last = mm(ps(n)[:, q % 2, 0:P * (q + 1)], QCs[s][:, h % 2, P * q:P * q + P],
                                      KCs[s][:, h % 2, 0:P * (q + 1)], start=True, stop=True)
                            if q % 2:
                                last.then_inc(full(n), 1)
                    if h:
                        g = h - 1
                        wait(pe, "p_ready", l, g + 1)
                        for kt in range(4):
                            n = f"t{'AB'[kt // 2]}{g}"
                            if kt % 2 == 0:
                                tile(l, n)
                            for q in range(kt, 4):
                                o = P * (q * (q + 1) // 2) + P * kt
                                last = nc.tensor.transpose(ps(n)[:, kt % 2, P * (q - kt):P * (q - kt) + P], PR[:, o:o + P], idt)
                            if kt % 2:
                                last.then_inc(full(n), 1)
                    def decode_step(name):
                        if name[:2] == "ds":
                            page_scores(int(name[2:]))
                        elif name == "dn":
                            tile(l, "dn")
                            mm(ps("dn")[0:NB, 0, 0:64], Z[:, Z_CKV, SEQ:T], flat(QL[:, :, :]), start=True, stop=False)
                            mm(ps("dn")[0:NB, 0, 0:64], Z[0:32, Z_KR, SEQ:T], QRB[0:32, :, 0, :], start=False, stop=True)\
                                .then_inc(full("dn"), 1)
                        elif name == "dm":
                            wait(pe, "m_all", l, 1)
                            wait_tile(pe, l, "dm")
                            settle(pe)
                            nc.tensor.transpose(ps("dm")[0:64, 0, 0:P], SMALL[:, 2, :], idt).then_inc(full("dm"), 1)
                        elif name == "db":
                            wait_emptied(pe, l, "dm")
                            tile(l, "db")
                            mm(ps("db")[:, 0, 0:64], const("ones", slice(0, 64)), SMALL[0:64, 7, :], start=True, stop=True)\
                                .then_inc(full("db"), 1)
                        elif name == "dd":
                            wait(pe, "rsum_ready", l, 1)
                            tile(l, "dd")
                            mm(ps("dd")[:, 0, 0:64], const("ones"), SMALL[:, 4, :], start=True, stop=True).then_inc(full("dd"), 1)
                        elif name[:2] == "dp":
                            b = int(name[2:])
                            s = b % 2
                            plain(pe)
                            wait_tile(pe, l, name)
                            pe.wait_ge(pages_in[s], l * per_layer + (NB // 2) * 16 * 2 * N_PAGES + (b // 2 + 1) * 16 * N_PAGES)
                            settle(pe)
                            mm(ps(name)[0:MH, 0, 0:P], SMALL[0:NB, 1, MH * b:MH * b + MH], C8[:, :], start=True, stop=False)
                            for j in range(N_PAGES):
                                o = (b * N_PAGES + j) * MH
                                last = mm(ps(name)[0:MH, 0, 0:P], PD[:, o:o + MH], KT[:, s, P * j:P * j + P],
                                          start=False, stop=j == N_PAGES - 1)
                            last.then_inc(full(name), 1)
                        else:
                            plain(pe)
                            wait_emptied(pe, l, "dp7")
                            wait_tile(pe, l, "dy")
                            settle(pe)
                            for b in range(NB):
                                last = nc.tensor.transpose(ps("dy")[:, 1, MH * b:MH * b + MH], O8[:, P * b:P * b + P],
                                                           const("ident", slice(0, MH), (0, MH)))
                            last.then_inc(S["ot_ready"][0], 1)

                    for name in DECODE_TILES[h]:
                        decode_step(name)
                    if h:
                        wait_emptied(pe, l, f"tA{g}")
                        wait_emptied(pe, l, f"tB{g}")
                        if g == 0:
                            wait_emptied(pe, l, "v23")
                        tile(l, f"o{g}")
                        for kt in range(4):
                            w = SEQ - P * kt
                            last = mm(ps(f"o{g}")[half(g), 0, P * kt:SEQ], V[:, kt, HD * g:HD * g + HD],
                                      PTR[:, off[kt]:off[kt] + w], start=(kt == 0), stop=(kt == 3))
                        last.then_inc(full(f"o{g}"), 1)
                wait(pe, "ol_ready", l, 1)
                plain(pe)
                for i in range(MH):
                    ol = SMALL[:, 6, :].rearrange("p (b h) -> p h b", b=NB)[:, i, :]
                    last = mm(ps("dy")[half(i), 0, NB * (i // 2):NB * (i // 2) + NB], UV[:, HD * i:HD * i + HD], ol,
                              start=True, stop=True)
                last.then_inc(full("dy"), 1)
                with pe.Fori(0, KD // 4) as it:
                    wait(pe, "mix_hi", l, 9)
                    wait(pe, "mix_lo", l, 4)
                    wait_emptied(pe, l, "dy")
                    for j in range(4):
                        product(l, f"wo{j}", [(U_OUT + j, KD)], xh, xl, it=it, per=4)
                norm_sum(l, "n2", KD)
                for hf, (j0, n) in enumerate(HALVES):
                    with pe.Fori(0, n // 2) as it:
                        for j in range(4):
                            product(l, f"up{hf}_{j}", [(U_UP[hf] + j, KD)], xh, xl, it=it, per=4,
                                    norm=KD if hf == j == 0 else None)
                    with pe.Fori(0, KD // 4) as it:
                        wait(pe, "hl_ready", l, j0 + n)
                        for m in range(4):
                            u = U_DN[hf] + 2 * m
                            product(l, f"dn{hf}_{m}", [(u, n // 2), (u + 1, n // 2)], lambda k: HH[:, k, :],
                                    lambda k: HL[:, k, :], it=it, per=8, chunks=j0 + n if m == 0 else None)
            norm_sum(DEPTH, "n1", 0)


DVE_LINKS = 93
CREDIT = 1
OUTS = [("y", (KD, P, T)), ("lat", (DEPTH, P, T)), ("rope", (DEPTH, 32, T)), ("ret", (DEPTH, P, 2 * HD)),
        ("gx", (DEPTH * RG, P, 11)), ("hr", (DEPTH * RG, P, NB + 1)), ("ff", (DEPTH, P, NJ, 10)),
        ("sret", (DEPTH, P, 2, NB * HD)), ("rgc0", (DEPTH, NB, RGC - 2, 256)), ("ffc0", (DEPTH, NB, 1, D_FF))]


def kernel(**inputs):
    import concourse.bacc as _bacc
    from concourse.bass_utils import run_bass_kernel_spmd as _run

    a = {k: np.asarray(v) for k, v in inputs.items()}
    D = DEPTH
    f32 = np.float32

    def unit(w, cols):
        d, rows, n = w.shape
        u = w.reshape(d, rows // P, P, n // cols, cols).transpose(0, 3, 2, 1, 4).reshape(d, n // cols, P, -1)
        return np.concatenate([u, np.zeros(u.shape[:3] + (UW - u.shape[3],), f32)], 3)

    w_in = a["w_in"]
    z_cols = [1280, 1024, 1152, 0, 1408, 128, 256, 384, 512, 640, 1440, 1568, 1696, 1824, 768, 896]
    parts = [unit(w_in[:, :, z_cols[z]:z_cols[z] + w], w) for z in ORDER for w in (32 if z == Z_KR else P,)]
    parts.append(unit(a["w_out"], P))
    up, dn = a["ffn_w_up"], a["ffn_w_down"]
    for j0, n in HALVES:
        g = unit(up[:, :, j0 * P:(j0 + n) * P], P)
        v = unit(up[:, :, D_FF + j0 * P:D_FF + (j0 + n) * P], P)
        parts.append(np.stack([g, v], 2).reshape(D, 2 * n, P, UW))
        m = n // 2
        two = [unit(dn[:, (j0 + i * m) * P:(j0 + (i + 1) * m) * P, :], P) for i in range(2)]
        parts.append(np.stack(two, 2).reshape(D, 2 * KD, P, UW))
    units = np.concatenate(parts, 1).reshape(D * N_UNITS, P, UW)

    cols = lambda x, n: x.reshape(D, n, P).transpose(0, 2, 1)
    par = {
        "n2": cols(a["norm2_w"], KD), "qn": cols(a["mla_q_norm_w"], 2),
        "kn": cols(a["mla_kv_norm_w"], 1), "gn": cols(a["ret_gn_w"], 2),
        "rcw": a["rg_conv_w"].reshape(D, RGC, RG, P).transpose(0, 3, 2, 1), "rcb": cols(a["rg_conv_b"], RG),
        "ba": cols(a["rg_b_a"], RG), "bx": cols(a["rg_b_x"], RG), "lam": cols(a["rg_lambda"], RG),
        "fcw": a["ffn_conv_w"].reshape(D, 3, NJ, P).transpose(0, 3, 1, 2), "fcb": cols(a["ffn_conv_b"], NJ),
        "cbuf": a["state_rg_conv"].reshape(D, NB, RGC - 1, RG, P).transpose(0, 4, 3, 2, 1),
        "h0": a["state_rglru"].reshape(D, NB, RG, P).transpose(0, 3, 2, 1),
        "fbuf": a["state_ffn_conv"].reshape(D, NB, 2, NJ, P).transpose(0, 4, 3, 2, 1),
    }
    par = np.concatenate([par[n].reshape(D, P, w) for n, w in PAR_W], 2)
    x = np.concatenate([a["x_prompt"].reshape(SEQ, D_MODEL), a["x_sample"].reshape(NB, D_MODEL)], 0)
    uq = a["mla_w_uq"].reshape(D, 2, P, MH, 96)
    uq = np.concatenate([uq[..., :64].reshape(D, 2, P, 512), uq[..., 64:].reshape(D, 2, P, 256)], 3)
    wg = np.zeros((D, P, 4, P), f32)
    for g, n in enumerate(("rg_w_a", "rg_w_x")):
        for blk in range(4):
            r = slice(64 * (blk % 2), 64 * (blk % 2) + 64)
            wg[:, r, 2 * g + blk // 2, r] = a[n][:, blk]
    lat = a["cache_mla_latent"]
    ins = {
        "units": units, "const": constants(), "par": par,
        "nw": np.concatenate([a["norm1_w"].reshape(D * KD, P), a["final_norm_w"].reshape(KD, P)]).T, "x": x.T.reshape(KD, P, T),
        "uq": uq.transpose(0, 2, 1, 3), "uk": a["mla_w_uk"].reshape(D, P, 512),
        "ukt": a["mla_w_uk"].transpose(0, 3, 2, 1), "uv": a["mla_w_uv"].reshape(D, P, 512), "wg": wg,
        "s0": a["state_ret"].reshape(D, NB, 2, 2, HD, HD).transpose(0, 3, 4, 2, 1, 5).reshape(D, P, 2, NB * HD),
        "kat": lat.transpose(0, 1, 3, 2).reshape(D * N_PHYS, P, P),
        "kar": a["cache_mla_krope"].transpose(0, 1, 3, 2).reshape(D * N_PHYS, 32, P),
        "ka": lat.reshape(D * N_PHYS, P, P), "pt": a["page_table"].reshape(1, NB * N_PAGES),
        "cp": a["state_rg_conv"][:, :, 1:], "fp": a["state_ffn_conv"][:, :, 1:],
    }
    nc = _bacc.Bacc("TRN2", target_bir_lowering=False, num_devices=1)
    arrays, args = {}, []
    for name, v in ins.items():
        v = np.ascontiguousarray(v)
        arrays[f"in_{name}"] = v
        args.append(nc.dram_tensor(f"in_{name}", v.shape, mybir.dt.from_np(v.dtype), kind="ExternalInput").ap())
    for name, shape in OUTS:
        args.append(nc.dram_tensor(f"out_{name}", shape, F32, kind="ExternalOutput").ap())
    build(nc, *args)
    r = _run(nc, [arrays], core_ids=[0]).results[0]
    o = {name: np.asarray(r[f"out_{name}"]) for name, _ in OUTS}

    y = o["y"].reshape(D_MODEL, T).T
    latT, ropeT = o["lat"].transpose(0, 2, 1), o["rope"].transpose(0, 2, 1)
    gx = o["gx"].reshape(D, RG * P, 11).transpose(0, 2, 1)
    hr = o["hr"].reshape(D, RG * P, NB + 1).transpose(0, 2, 1)
    ff = o["ff"].transpose(0, 3, 2, 1).reshape(D, 10, D_FF)
    ret = o["ret"].reshape(D, 2, HD, 2, HD).transpose(0, 3, 1, 2, 4).reshape(D, 1, RH, HD, HD)
    sret = o["sret"].reshape(D, 2, HD, 2, NB, HD).transpose(0, 4, 3, 1, 2, 5).reshape(D, NB, RH, HD, HD)
    c = np.ascontiguousarray
    return (c(y[None, :SEQ]), c(y[SEQ:, None]), c(latT[:, None, :SEQ]), c(ropeT[:, None, :SEQ]), c(ret),
            c(gx[:, None, 0:3]), c(hr[:, None, 0]), c(ff[:, None, 0:2]), c(latT[:, SEQ:, None]), c(ropeT[:, SEQ:, None]),
            c(sret), np.concatenate([o["rgc0"], gx[:, 3:, None]], 2), c(hr[:, 1:]),
            np.concatenate([o["ffc0"], ff[:, 2:, None]], 2))
```
